# Optimizing a Trainium2 kernel written in Bass

```python
import math
import jax
import jax.numpy as jnp
from jax import lax
import numpy as np

D_MODEL = 2048
BATCH = 1
SEQ = 256
DEPTH = 2
DEC_BATCH = 8
DEC_SEQ = 1
PAST_LEN = 2048
PAGE_SIZE = 128

HEAD_DIM = 128
N_MIX_HEADS = D_MODEL // HEAD_DIM
N_MEM_HEADS = 4
N_SELF_HEADS = N_MIX_HEADS - N_MEM_HEADS
KV_A = 2
G_A = N_SELF_HEADS // KV_A
KV_B = 4
G_B = N_SELF_HEADS // KV_B
IDX_HEADS = 16
IDX_DIM = 64
TOPK_MAX = 256
N_MEM = 256
N_GROUPS = 4
EXPERTS_PER_GROUP = 4
N_EXPERTS = N_GROUPS * EXPERTS_PER_GROUP
TOP_IN_GROUP = 2
D_EXPERT = D_MODEL // 4
Q_BLOCK = 128
N_A_LAYERS = (DEPTH + 1) // 2
N_B_LAYERS = DEPTH // 2
DN_ALPHA = (2 * DEPTH) ** 0.25
DN_BETA = (8 * DEPTH) ** -0.25
LN_EPS = 1e-5
NEG_INF = -1e30
FORGET_BIAS = 4.0

QS = N_SELF_HEADS * HEAD_DIM
QM = N_MEM_HEADS * HEAD_DIM
KA = KV_A * HEAD_DIM
KB = KV_B * HEAD_DIM
QI = IDX_HEADS * IDX_DIM
SPLIT_A = (QS, QS + KA, QS + 2 * KA, QS + 2 * KA + QI, QS + 2 * KA + QI + IDX_DIM,
           QS + 2 * KA + QI + IDX_DIM + IDX_HEADS)
COLS_A = SPLIT_A[-1] + QM
SPLIT_B = (QS, QS + KB, QS + 2 * KB, QS + 2 * KB + N_SELF_HEADS)
COLS_B = SPLIT_B[-1] + QM

kernel_name = "hybrid_dsa_fox_memory_hmoe_step"

F32 = jnp.float32

def alibi_slopes(n):
    def pow2(m):
        start = 2.0 ** (-8.0 / m)
        return [start ** (i + 1) for i in range(m)]
    if math.log2(n).is_integer():
        s = pow2(n)
    else:
        c = 2 ** math.floor(math.log2(n))
        s = pow2(c) + pow2(2 * c)[0::2][: n - c]
    return jnp.asarray(s, F32)

def layer_norm(x, g, b):
    xf = x.astype(F32)
    mu = jnp.mean(xf, -1, keepdims=True)
    var = jnp.mean(jnp.square(xf - mu), -1, keepdims=True)
    return ((xf - mu) * lax.rsqrt(var + LN_EPS) * g + b).astype(x.dtype)

def proj_a(h, w_in):
    B, T, _ = h.shape
    q, k, v, qi, ki, wi, qm = jnp.split(h @ w_in, SPLIT_A, axis=-1)
    return (q.reshape(B, T, N_SELF_HEADS, HEAD_DIM), k.reshape(B, T, KV_A, HEAD_DIM),
            v.reshape(B, T, KV_A, HEAD_DIM), qi.reshape(B, T, IDX_HEADS, IDX_DIM), ki, wi,
            qm.reshape(B, T, N_MEM_HEADS, HEAD_DIM))

def proj_b(h, w_in, b_f):
    B, T, _ = h.shape
    q, k, v, f, qm = jnp.split(h @ w_in, SPLIT_B, axis=-1)
    logf = jax.nn.log_sigmoid(f.astype(F32) + b_f)
    return (q.reshape(B, T, N_SELF_HEADS, HEAD_DIM), k.reshape(B, T, KV_B, HEAD_DIM),
            v.reshape(B, T, KV_B, HEAD_DIM), logf, qm.reshape(B, T, N_MEM_HEADS, HEAD_DIM))

def indexer_scores(qi, wi, ki):
    s = jnp.einsum('qhd,ld->qlh', qi, ki).astype(F32) * (IDX_DIM ** -0.5)
    return jnp.einsum('qlh,qh->ql', jax.nn.relu(s), wi.astype(F32) * (IDX_HEADS ** -0.5))

def sparse_attend(q, k_sel, v_sel, pos_q, pos_sel, slopes):
    tq = q.shape[0]
    qg = q.reshape(tq, KV_A, G_A, HEAD_DIM)
    s = jnp.einsum('qkgd,qnkd->qkgn', qg, k_sel).astype(F32) * (HEAD_DIM ** -0.5)
    dist = (pos_q[:, None] - pos_sel).astype(F32)
    s = s - slopes.reshape(KV_A, G_A)[None, :, :, None] * dist[:, None, None, :]
    s = jnp.where((pos_sel <= pos_q[:, None])[:, None, None, :], s, NEG_INF)
    p = jax.nn.softmax(s, axis=-1).astype(v_sel.dtype)
    o = jnp.einsum('qkgn,qnkd->qkgd', p, v_sel)
    return o.reshape(tq, N_SELF_HEADS, HEAD_DIM)

def dsa_prompt(q, k, v, qi, ki, wi, slopes):
    B, S = q.shape[:2]
    nb = S // Q_BLOCK
    topk = min(TOPK_MAX, S // 4)
    pos_k = jnp.arange(S)

    def blk(args):
        b, j = args
        t0 = j * Q_BLOCK
        sl = lambda a: lax.dynamic_slice_in_dim(a[b], t0, Q_BLOCK, axis=0)
        pos_q = t0 + jnp.arange(Q_BLOCK)
        sc = indexer_scores(sl(qi), sl(wi), ki[b])
        sc = jnp.where(pos_k[None, :] <= pos_q[:, None], sc, NEG_INF)
        _, sel = lax.top_k(sc, topk)
        kb, vb = k[b], v[b]
        return sparse_attend(sl(q), kb[sel], vb[sel], pos_q, sel, slopes)

    bb, jj = jnp.meshgrid(jnp.arange(B), jnp.arange(nb), indexing='ij')
    out = lax.map(blk, (bb.reshape(-1), jj.reshape(-1)))
    return out.reshape(B, S, N_SELF_HEADS, HEAD_DIM)

def dsa_sample(q, k_new, v_new, qi, ki_new, wi, pool_k, pool_v, pool_ki, page_table, slopes):
    Bd, T = q.shape[:2]
    P = page_table.shape[1] * PAGE_SIZE
    L = P + T
    topk = min(TOPK_MAX, L // 4)
    ki_past = pool_ki[page_table].reshape(Bd, P, IDX_DIM)
    ki_all = jnp.concatenate([ki_past, ki_new.astype(ki_past.dtype)], axis=1)
    pos_q = P + jnp.arange(T)
    pos_k = jnp.arange(L)
    sc = jax.vmap(indexer_scores)(qi, wi, ki_all)
    sc = jnp.where(pos_k[None, None, :] <= pos_q[None, :, None], sc, NEG_INF)
    _, sel = lax.top_k(sc, topk)
    is_new = sel >= P
    past_pos = jnp.minimum(sel, P - 1)
    phys = jnp.take_along_axis(page_table, (past_pos // PAGE_SIZE).reshape(Bd, -1),
                               axis=1).reshape(sel.shape)
    off = past_pos % PAGE_SIZE
    new_i = jnp.clip(sel - P, 0, T - 1)
    bidx = jnp.arange(Bd)[:, None, None]

    def pick(pool, new):
        old = pool[phys, off]
        nw = new[bidx, new_i].astype(old.dtype)
        return jnp.where(is_new[..., None, None], nw, old)

    k_sel = pick(pool_k, k_new)
    v_sel = pick(pool_v, v_new)
    return jax.vmap(sparse_attend, in_axes=(0, 0, 0, None, 0, None))(
        q, k_sel, v_sel, pos_q, sel, slopes)

def fox_attend(qg, k, v, c_q, c_k, pos_q, pos_k):
    B, Tq = qg.shape[:2]
    s = jnp.einsum('bqkgd,blkd->bkgql', qg, k).astype(F32) * (HEAD_DIM ** -0.5)
    s = s + c_q.transpose(0, 2, 3, 1)[..., None] - c_k.transpose(0, 2, 3, 1)[..., None, :]
    s = jnp.where(pos_k[None, :] <= pos_q[:, None], s, NEG_INF)
    p = jax.nn.softmax(s, axis=-1).astype(v.dtype)
    o = jnp.einsum('bkgql,blkd->bqkgd', p, v)
    return o.reshape(B, Tq, N_SELF_HEADS, HEAD_DIM)

def fox_prompt(q, k, v, logf):
    B, S = q.shape[:2]
    c = jnp.cumsum(logf.astype(F32), axis=1)
    qg = q.reshape(B, S, KV_B, G_B, HEAD_DIM)
    cg = c.reshape(B, S, KV_B, G_B)
    pos_k = jnp.arange(S)

    def blk(j):
        t0 = j * Q_BLOCK
        qb = lax.dynamic_slice_in_dim(qg, t0, Q_BLOCK, axis=1)
        cb = lax.dynamic_slice_in_dim(cg, t0, Q_BLOCK, axis=1)
        return fox_attend(qb, k, v, cb, cg, t0 + jnp.arange(Q_BLOCK), pos_k)

    out = lax.map(blk, jnp.arange(S // Q_BLOCK))
    return out.transpose(1, 0, 2, 3, 4).reshape(B, S, N_SELF_HEADS, HEAD_DIM)

def fox_sample(q, k_new, v_new, logf_new, pool_k, pool_v, pool_lf, page_table):
    Bd, T = q.shape[:2]
    P = page_table.shape[1] * PAGE_SIZE
    L = P + T
    k_all = jnp.concatenate([pool_k[page_table].reshape(Bd, P, KV_B, HEAD_DIM),
                             k_new.astype(pool_k.dtype)], axis=1)
    v_all = jnp.concatenate([pool_v[page_table].reshape(Bd, P, KV_B, HEAD_DIM),
                             v_new.astype(pool_v.dtype)], axis=1)
    lf_all = jnp.concatenate([pool_lf[page_table].reshape(Bd, P, N_SELF_HEADS).astype(F32),
                              logf_new.astype(F32)], axis=1)
    cg = jnp.cumsum(lf_all, axis=1).reshape(Bd, L, KV_B, G_B)
    qg = q.reshape(Bd, T, KV_B, G_B, HEAD_DIM).astype(k_all.dtype)
    return fox_attend(qg, k_all, v_all, cg[:, P:], cg, P + jnp.arange(T), jnp.arange(L))

def mem_attend(qm, mk, mv):
    s = jnp.einsum('bqhd,bmhd->bhqm', qm, mk.astype(qm.dtype)).astype(F32) * (HEAD_DIM ** -0.5)
    p = jax.nn.softmax(s, axis=-1).astype(qm.dtype)
    return jnp.einsum('bhqm,bmhd->bqhd', p, mv.astype(qm.dtype))

def hier_moe(h, w_r1, b_r1, w_r2, b_r2, w_gate, w_up, w_down):
    B, T, D = h.shape
    xt = h.reshape(B * T, D)
    n = xt.shape[0]
    g_prob = jax.nn.softmax((xt @ w_r1).astype(F32) + b_r1, axis=-1)
    p_grp, grp = lax.top_k(g_prob, 1)
    e_all = jnp.einsum('nd,gde->nge', xt, w_r2).astype(F32) + b_r2
    e_logit = jnp.take_along_axis(e_all, grp[:, :, None], axis=1)[:, 0]
    p_e, e_idx = lax.top_k(jax.nn.softmax(e_logit, axis=-1), TOP_IN_GROUP)
    p_e = p_e / jnp.sum(p_e, -1, keepdims=True)
    expert = grp * EXPERTS_PER_GROUP + e_idx
    gate = jnp.zeros((n, N_EXPERTS), F32).at[jnp.arange(n)[:, None], expert].add(p_grp * p_e)
    hid = jax.nn.silu(jnp.einsum('nd,edf->nef', xt, w_gate)) * jnp.einsum('nd,edf->nef', xt, w_up)
    y = jnp.einsum('nef,efd->nd', hid * gate[:, :, None].astype(hid.dtype), w_down)
    return y.reshape(B, T, D)

def residual_block(h, so, mo, w_o, g1, b1, g2, b2, w_r1, b_r1, w_r2, b_r2, w_gate, w_up, w_down):
    B, T, _ = h.shape
    mix = jnp.concatenate([so.reshape(B, T, QS), mo.reshape(B, T, QM).astype(so.dtype)], -1) @ w_o
    h = layer_norm(DN_ALPHA * h + mix, g1, b1)
    return layer_norm(DN_ALPHA * h + hier_moe(h, w_r1, b_r1, w_r2, b_r2, w_gate, w_up, w_down), g2, b2)

def setup_inputs(seed: int = 0) -> dict:
    key = jax.random.key(seed)
    ks = iter(jax.random.split(key, 40))
    nrm = lambda shape, scale=1.0: jax.random.normal(next(ks), shape, F32) * scale
    n_pages = PAST_LEN // PAGE_SIZE
    n_pool = (5 * DEC_BATCH * n_pages) // 4
    page_table = jax.random.permutation(next(ks), n_pool)[: DEC_BATCH * n_pages].reshape(
        DEC_BATCH, n_pages).astype(jnp.int32)
    col_a = jnp.ones((COLS_A,), F32).at[QS + KA:QS + 2 * KA].set(DN_BETA)
    col_b = jnp.ones((COLS_B,), F32).at[QS + KB:QS + 2 * KB].set(DN_BETA)
    col_m = jnp.ones((2 * QM,), F32).at[QM:].set(DN_BETA)
    sd = D_MODEL ** -0.5
    return {
        "x_prompt": nrm((BATCH, SEQ, D_MODEL)),
        "x_sample": nrm((DEC_BATCH, DEC_SEQ, D_MODEL)),
        "mem_prompt": nrm((BATCH, N_MEM, D_MODEL)),
        "cache_a_k": nrm((N_A_LAYERS, n_pool, PAGE_SIZE, KV_A, HEAD_DIM)),
        "cache_a_v": nrm((N_A_LAYERS, n_pool, PAGE_SIZE, KV_A, HEAD_DIM), DN_BETA),
        "cache_a_ik": nrm((N_A_LAYERS, n_pool, PAGE_SIZE, IDX_DIM)),
        "cache_b_k": nrm((N_B_LAYERS, n_pool, PAGE_SIZE, KV_B, HEAD_DIM)),
        "cache_b_v": nrm((N_B_LAYERS, n_pool, PAGE_SIZE, KV_B, HEAD_DIM), DN_BETA),
        "cache_b_lf": jax.nn.log_sigmoid(nrm((N_B_LAYERS, n_pool, PAGE_SIZE, N_SELF_HEADS)) + FORGET_BIAS),
        "cache_mem_k": nrm((DEPTH, DEC_BATCH, N_MEM, N_MEM_HEADS, HEAD_DIM)),
        "cache_mem_v": nrm((DEPTH, DEC_BATCH, N_MEM, N_MEM_HEADS, HEAD_DIM), DN_BETA),
        "page_table": page_table,
        "w_in_a": nrm((N_A_LAYERS, D_MODEL, COLS_A), sd) * col_a,
        "w_in_b": nrm((N_B_LAYERS, D_MODEL, COLS_B), sd) * col_b,
        "b_f": FORGET_BIAS + nrm((N_B_LAYERS, N_SELF_HEADS), 0.5),
        "w_mem_kv": nrm((DEPTH, D_MODEL, 2 * QM), sd) * col_m,
        "w_o": nrm((DEPTH, QS + QM, D_MODEL), (QS + QM) ** -0.5 * DN_BETA),
        "ln1_g": 1.0 + nrm((DEPTH, D_MODEL), 0.02),
        "ln1_b": nrm((DEPTH, D_MODEL), 0.02),
        "ln2_g": 1.0 + nrm((DEPTH, D_MODEL), 0.02),
        "ln2_b": nrm((DEPTH, D_MODEL), 0.02),
        "w_r1": nrm((DEPTH, D_MODEL, N_GROUPS), sd),
        "b_r1": nrm((DEPTH, N_GROUPS), 0.01),
        "w_r2": nrm((DEPTH, N_GROUPS, D_MODEL, EXPERTS_PER_GROUP), sd),
        "b_r2": nrm((DEPTH, N_GROUPS, EXPERTS_PER_GROUP), 0.01),
        "w_gate": nrm((DEPTH, N_EXPERTS, D_MODEL, D_EXPERT), sd),
        "w_up": nrm((DEPTH, N_EXPERTS, D_MODEL, D_EXPERT), sd),
        "w_down": nrm((DEPTH, N_EXPERTS, D_EXPERT, D_MODEL), D_EXPERT ** -0.5 * DN_BETA),
    }

def reference(x_prompt, x_sample, mem_prompt, cache_a_k, cache_a_v, cache_a_ik, cache_b_k,
              cache_b_v, cache_b_lf, cache_mem_k, cache_mem_v, page_table, w_in_a, w_in_b, b_f,
              w_mem_kv, w_o, ln1_g, ln1_b, ln2_g, ln2_b, w_r1, b_r1, w_r2, b_r2, w_gate, w_up,
              w_down):
    slopes = alibi_slopes(N_SELF_HEADS)
    hp, hs = x_prompt, x_sample
    Bp = hp.shape[0]
    a_k_p, a_v_p, a_ik_p, a_k_s, a_v_s, a_ik_s = [], [], [], [], [], []
    b_k_p, b_v_p, b_lf_p, b_k_s, b_v_s, b_lf_s = [], [], [], [], [], []
    mem_k_p, mem_v_p = [], []
    for i in range(DEPTH):
        j = i // 2
        mkv = (mem_prompt @ w_mem_kv[i]).reshape(Bp, N_MEM, 2, N_MEM_HEADS, HEAD_DIM)
        mk_p, mv_p = mkv[:, :, 0], mkv[:, :, 1]
        mem_k_p.append(mk_p)
        mem_v_p.append(mv_p)
        if i % 2 == 0:
            q, k, v, qi, ki, wi, qm = proj_a(hp, w_in_a[j])
            so_p = dsa_prompt(q, k, v, qi, ki, wi, slopes)
            mo_p = mem_attend(qm, mk_p, mv_p)
            a_k_p.append(k)
            a_v_p.append(v)
            a_ik_p.append(ki)
            q, k, v, qi, ki, wi, qm = proj_a(hs, w_in_a[j])
            so_s = dsa_sample(q, k, v, qi, ki, wi, cache_a_k[j], cache_a_v[j], cache_a_ik[j],
                              page_table, slopes)
            mo_s = mem_attend(qm, cache_mem_k[i], cache_mem_v[i])
            a_k_s.append(k)
            a_v_s.append(v)
            a_ik_s.append(ki)
        else:
            q, k, v, lf, qm = proj_b(hp, w_in_b[j], b_f[j])
            so_p = fox_prompt(q, k, v, lf)
            mo_p = mem_attend(qm, mk_p, mv_p)
            b_k_p.append(k)
            b_v_p.append(v)
            b_lf_p.append(lf)
            q, k, v, lf, qm = proj_b(hs, w_in_b[j], b_f[j])
            so_s = fox_sample(q, k, v, lf, cache_b_k[j], cache_b_v[j], cache_b_lf[j], page_table)
            mo_s = mem_attend(qm, cache_mem_k[i], cache_mem_v[i])
            b_k_s.append(k)
            b_v_s.append(v)
            b_lf_s.append(lf)
        hp = residual_block(hp, so_p, mo_p, w_o[i], ln1_g[i], ln1_b[i], ln2_g[i], ln2_b[i],
                            w_r1[i], b_r1[i], w_r2[i], b_r2[i], w_gate[i], w_up[i], w_down[i])
        hs = residual_block(hs, so_s.astype(hs.dtype), mo_s, w_o[i], ln1_g[i], ln1_b[i], ln2_g[i],
                            ln2_b[i], w_r1[i], b_r1[i], w_r2[i], b_r2[i], w_gate[i], w_up[i],
                            w_down[i])
    return (hp, hs,
            jnp.stack(a_k_p), jnp.stack(a_v_p), jnp.stack(a_ik_p),
            jnp.stack(b_k_p), jnp.stack(b_v_p), jnp.stack(b_lf_p),
            jnp.stack(mem_k_p), jnp.stack(mem_v_p),
            jnp.stack(a_k_s), jnp.stack(a_v_s), jnp.stack(a_ik_s),
            jnp.stack(b_k_s), jnp.stack(b_v_s), jnp.stack(b_lf_s))


_drawn_inputs = setup_inputs


def setup_inputs(seed=0):
    import zlib

    import numpy as np

    out = dict(_drawn_inputs(seed))
    spreads = {}
    factors = {'cache_b_lf': 30.025,
     'cache_mem_k': 5.252,
     'cache_mem_v': 4.027,
     'b_r1': 7.895,
     'b_r2': 21.841}
    for name, (base, spread) in spreads.items():
        noise = np.random.default_rng([zlib.crc32(name.encode()), seed]).standard_normal(out[name].shape)
        drawn = base * np.exp(spread * noise) if base else spread * noise
        out[name] = jnp.asarray(drawn.astype(out[name].dtype))
    for name, factor in factors.items():
        out[name] = (out[name] * factor).astype(out[name].dtype)
    return out
```

```python
import concourse.bass as bass
from concourse import mybir
from contextlib import ExitStack
import numpy as np

F32 = mybir.dt.float32
I32 = mybir.dt.int32
ALU = mybir.AluOpType
ACT = mybir.ActivationFunctionType
AX = mybir.AxisListType

P = 128
D = 2048
KC = D // P
SEQ = 256
NB = 8
T = SEQ + NB
PAGES = 16
PAST = PAGES * P
L1 = PAST + 1
N_POOL = 160
H = 12
HM = 4
IH = 16
TOPK_P, TOPK_S = 64, 256
SCALE = float(np.float32(P ** -0.5))
NEG = -1e30
TAKEN = -3e38
ALPHA = 4 ** 0.25
EPS = 1e-5
NE = 16
FE = 512
CAP = 64
PAIRS = NE // 2
MAX_EXTRA = 2 * T // (CAP + 1)
ENTRIES = 2 * (PAIRS + (MAX_EXTRA + 1) // 2 + 1)
CHUNKS = -(-T // CAP) - 1
RING, UNIT = 6, 4096
COLS_A, COLS_B = 3664, 3084

CONST = {}


def const_table():
    parts, at = [], 0

    def add(name, a):
        nonlocal at
        full = np.zeros((P, a.shape[1]), np.float32)
        full[:a.shape[0]] = a
        CONST[name] = (at, a.shape[1])
        parts.append(full)
        at += a.shape[1]

    i = np.arange(P)
    add("ident", np.eye(P))
    add("mean", np.full((P, P), 1.0 / D))
    add("ones", np.ones((P, P)))
    add("before", (i[:, None] < i[None, :]).astype(np.float32))
    k = np.arange(SEQ)
    add("causal", np.concatenate([np.where(k[None] <= (i + P * t)[:, None], 0.0, NEG) for t in range(2)], 1))
    add("dist", np.concatenate([(i + P * t)[:, None] - k[None] for t in range(2)], 1))
    add("slot", np.broadcast_to(np.arange(CAP), (P, CAP)))
    rep16 = np.zeros((IH, P))
    rep16[np.arange(P) % IH, i] = 1
    add("rep16", rep16)
    add("own16", (i[:, None] // IH == np.arange(NB)[None]).astype(np.float32))
    r = np.arange(NB * H)
    rep12 = np.zeros((H, NB * H))
    rep12[r % H, r] = 1
    add("rep12", rep12)
    own12 = (r[:, None] // H == np.arange(NB)[None]).astype(np.float32)
    add("own12", own12)
    to12 = np.zeros((P, NB * H))
    to12[96:96 + NB] = own12.T
    add("to12", to12)
    add("first", np.broadcast_to(np.tile([4.0, 3.0, 2.0, 1.0], 3), (P, 12)))
    add("valid", np.stack([np.ones(P), np.ones(P), i < NB], 1))
    e, c = np.divmod(np.arange(NE * CHUNKS), CHUNKS)
    add("chunk_base", np.broadcast_to(CAP * (c + 1.0), (P, NE * CHUNKS)))
    add("chunk_expert", np.broadcast_to(e.astype(np.float32), (P, NE * CHUNKS)))
    add("entry_expert", np.broadcast_to(np.where(np.arange(ENTRIES) < NE, np.arange(ENTRIES), 0), (P, ENTRIES)))
    add("entry", np.broadcast_to(np.arange(ENTRIES - NE), (P, ENTRIES - NE)))
    return np.concatenate(parts, 1).astype(np.float32)


def slopes():
    def pow2(m):
        return [(2.0 ** (-8.0 / m)) ** (j + 1) for j in range(m)]
    return pow2(8) + pow2(16)[0::2][:H - 8]


def alibi_rows():
    s = np.tile(np.asarray(slopes(), np.float32), NB)
    return -(s[:, None] * (PAST - np.arange(L1, dtype=np.float32))[None]).astype(np.float32)


CONSTS = const_table()
NC_CONST = CONSTS.shape[1]
BIG = 4096.0


class Ring:

    def __init__(self, start=0):
        self.n = start
        self.full = [0] * RING
        self.used = [0] * RING

    def take(self, n_dma=1):
        s = self.n % RING
        self.n += 1
        before = self.used[s]
        self.full[s] += 16 * n_dma
        self.used[s] += 1
        return s, self.full[s], self.used[s], before


def plan(layer):
    u = []
    if layer == 0:
        u += [("ln", 0, 5), ("x", 0, 1), ("xs", 0, 1), ("kiwi", 0, 2), ("qi", 0, 1), ("qi", 1, 1), ("qi", 2, 1),
              ("qi", 3, 1), ("ik", 0, 64), ("ik", 1, 64)]
    else:
        u += [("f", 0, 1)]
    u += [("q", k, 1) for k in range(6)]
    u += [("kv", k, 1) for k in range(2 if layer == 0 else 4)]
    u += [("qm", k, 1) for k in range(2)]
    if layer == 1:
        u += [("lf", 0, 128)]
    u += [("mem", 0, 1)] + [("mkv", k, 1) for k in range(4)]
    n = 8 if layer == 0 else 16
    u += [("k", k, 128 // n) for k in range(n)] + [("mk", k, 4) for k in range(2)]
    u += [("v", k, 128 // n) for k in range(n)] + [("mv", k, 4) for k in range(2)]
    u += [("r", 0, 5)] + [("o", k, 1) for k in range(8)]
    return u


def step_kernel(nc, i, o):
    with ExitStack() as ctx:
        sems = {}

        def S(name):
            if name not in sems:
                sems[name] = ctx.enter_context(nc.semaphore(name))
            return sems[name]

        def sb(name, cols, dt=F32, rows=P):
            return ctx.enter_context(nc.sbuf_tensor(name, [rows, cols], dt))

        ring = [sb(f"ring{k}", UNIT) for k in range(RING)]
        X = sb("X", KC * T)
        AT = sb("AT", KC * T)
        consts = sb("consts", NC_CONST)
        lnp = sb("lnp", 128)
        rbias = sb("rbias", 2, rows=20)
        fbias = sb("fbias", 1, rows=H)
        ptab = sb("ptab", NB * PAGES, I32, rows=1)
        wr = sb("wr", KC * 20)
        ARENA = 17416
        arena = sb("arena", ARENA)
        B = [ctx.enter_context(nc.psum_tensor(f"bank{k}", [P, 512], F32)) for k in range(8)]

        def cst(name, rows=P, lo=0):
            a, n = CONST[name]
            return consts[lo:lo + rows, a:a + n]

        ident = cst("ident")

        def ar(at, n, rows=P):
            return arena[0:rows, at:at + n]

        Xc = [X[:, c * T:(c + 1) * T] for c in range(KC)]
        Ac = [AT[:, c * T:(c + 1) * T] for c in range(KC)]
        Xv = X[:, :].rearrange("p (c t) -> p c t", t=T)
        Av = AT[:, :].rearrange("p (c t) -> p c t", t=T)

        class Lay:
            pass

        lay = []
        for layer in range(2):
            a = Lay()
            nk = a.nk = 2 if layer == 0 else 4
            a.G = H // nk
            a.W = nk * P
            at = 0

            def place(n, rows=P):
                nonlocal at
                at += n
                assert at <= ARENA, at
                return ar(at - n, n, rows)

            a.qT = place(H * T)
            a.PT = ar(0, PAGES * 96)
            a.PTm = ar(PAGES * 96, 64)
            a.PTn = ar(PAGES * 96 + 64, 96, NB)
            a.epn = ar(PAGES * 96 + 160, NB, 96)
            a.qmT = place(HM * T)
            a.kT = place(nk * T)
            if layer == 0:
                a.vT = place(nk * T)
            a.VN = place(2 * a.W)
            a.VNs = place(a.W, NB)
            a.memK = place(HM * SEQ)
            a.memV = place(2 * 512)
            a.S = place(L1 + 3)
            if layer == 1:
                a.vT = a.S[:, 0:nk * T]
            a.KTs = place(1024)
            a.KN = a.KTs
            a.Qz = place(3072)
            a.qiT = a.Qz
            a.sc = [a.Qz[:, 512 * k:512 * k + 512] for k in range(2)]
            a.PTp = [a.Qz[:, 1024 + 512 * k:1536 + 512 * k] for k in range(2)]
            a.Qmz = place(HM * NB * 32)
            a.QIz = a.Qmz
            a.mvT = a.Qmz
            a.Sm = place(SEQ, 32)
            if layer == 0:
                kiwi = place(2 * T)
                a.KI, a.WI = kiwi[:, 0:T], kiwi[0:IH, T:2 * T]
                a.KNs = kiwi[0:NB, 0:512]
                a.ovs = kiwi[0:H, 0:512]
                a.nat = place(224)
                a.MASK = place(512)
                a.tb = place(512)
                a.RL = a.memV
                a.Wb = place(NB)
                a.m8 = place(8)
            else:
                a.ovs = place(512, H)
                a.KNs = a.ovs[0:NB, :]
                a.fx = place(T, H)
                a.fe = place(T, H)
                a.cq = place(24)
                a.lfn = place(36)
                a.own = place(NB, 96)
            a.st = place(16)
            lay.append(a)

        M = Lay()
        at = 0
        M.xtok = ar(at, 3 * D); at += 3 * D
        M.xsT = ar(at, KC * P); at += KC * P
        M.ys = ar(at, D); at += D
        M.sel = ar(at, 3 * P); at += 3 * P
        M.sg = ar(at, 3 * P); at += 3 * P
        M.gt = ar(at, T); at += T
        M.ex = ar(at, 512); at += 512
        M.hh = ar(at, 512); at += 512
        M.hT = ar(at, 512); at += 512
        M.sq = [ar(at, T), ar(at + T, T)]; at += 2 * T
        M.rstd = ar(at, T); at += T
        M.lgT = ar(at, T, 20); at += T
        M.lg = ar(at, 60); at += 60
        M.a4 = [ar(at + 12 * k, 12) for k in range(8)]; at += 96
        M.w16 = [ar(at + 48 * k, 48) for k in range(4)]; at += 192
        M.c1 = [ar(at + 3 * k, 3) for k in range(12)]; at += 36
        M.cnt = ar(at, 16); at += 16
        M.fl = [ar(at + 64 * k, 64) for k in range(4)]; at += 256
        M.LB = ar(at, ENTRIES); at += ENTRIES
        M.LE = ar(at, ENTRIES); at += ENTRIES
        NX = ENTRIES - NE
        M.ind = ar(at, NX * NE * CHUNKS); at += NX * NE * CHUNKS
        M.d3 = ar(at, 6); at += 6
        M.no = ar(at, 8); at += 8
        assert at <= ARENA, at
        ent = sb("entries", ENTRIES, I32, rows=1)
        npair = sb("npair", 1, I32, rows=1)

        units = []
        starts = []
        r = Ring()
        moe_at = []
        for layer in range(2):
            if layer:
                r = Ring(r.n + 12 * PAIRS)
            at_l = {}
            for name, k, n in plan(layer):
                at_l[name, k] = r.take(n)
            units.append(at_l)
            moe_at.append((r.n, list(r.full), list(r.used)))
            r.n += 0

        def full(layer, s):
            return S(f"full{s}_l{layer}")

        def free(layer, s):
            return S(f"free{s}_l{layer}")

        def arrived(eng, layer, name, k=0):
            s, v, _, _ = units[layer][name, k]
            eng.wait_ge(full(layer, s), v)
            return ring[s]

        def leave(mm, layer, name, k=0):
            mm.then_inc(free(layer, units[layer][name, k][0]), 1)

        def left(eng, layer, name, k=0):
            s, _, v, _ = units[layer][name, k]
            eng.wait_ge(free(layer, s), v)

        def moe_unit(layer, k, it):
            n0, f0, u0 = moe_at[layer]
            s = (n0 + k) % RING
            return s, it * 32 + (f0[s] + 16 * (k // RING + 1)), it * 2 + (u0[s] + k // RING + 1)

        block = ctx.enter_context(nc.Block())

        @block.sync
        def _(sp):
            sp.dma_start(consts[:, :], i["consts"]).then_inc(S("consts_in"), 16)
            sp.dma_start(ptab[:, :], i["page_table"].rearrange("(a b) c -> a (b c)", a=1)).then_inc(S("table_in"), 16)
            for layer in range(2):
                sp.dma_start(rbias[0:4, layer:layer + 1],
                             i["b_r1"][layer].rearrange("(a b) -> a b", b=1)).then_inc(S("bias_in"), 16)
                sp.dma_start(rbias[4:20, layer:layer + 1],
                             i["b_r2"][layer].rearrange("g (e b) -> (g e) b", b=1)).then_inc(S("bias_in"), 16)
            sp.dma_start(fbias[:, :], i["b_f"][0].rearrange("(a b) -> a b", b=1)).then_inc(S("bias_in"), 16)
            sp.wait_ge(S("table_in"), 16)
            pregs = [sp.alloc_register(f"page{k}") for k in range(8)]

            def pages(layer, s, b, first, n, cache, dst):
                for g in range(first, first + n, 8):
                    sp.reg_load(pregs, ptab[0:1, b * PAGES + g:b * PAGES + g + 8])
                    for k in range(8):
                        page = sp.snap(pregs[k], min_val=0, max_val=N_POOL - 1)
                        sp.dma_start(dst(g + k), cache[bass.ds(page, 1)].rearrange("a p w -> (a p) w"))\
                          .then_inc(full(layer, s), 16)

            def wload(layer, s, w, half, c0, n, at=0, width=None):
                width = width or n
                rows = w.rearrange("(c p) f -> p c f", p=P)
                k = KC // 2 if half is not None else KC
                c = (half or 0) * k
                dst = ring[s][:, 0:k * width].rearrange("p (c f) -> p c f", f=width)[:, :, at:at + n]
                sp.dma_start(dst, rows[:, c:c + k, c0:c0 + n]).then_inc(full(layer, s), 16)

            for layer in range(2):
                win = i["w_in_a"][0] if layer == 0 else i["w_in_b"][0]
                ck = i["cache_a_k" if layer == 0 else "cache_b_k"][0].rearrange("n p k d -> n p (k d)")
                cv = i["cache_a_v" if layer == 0 else "cache_b_v"][0].rearrange("n p k d -> n p (k d)")
                W = 256 if layer == 0 else 512
                col_kv, col_qm = H * P, (COLS_A if layer == 0 else COLS_B) - HM * P
                if layer == 1:
                    sp.wait_ge(S("route_done_l0"), 1)
                    n_pair = sp.value_load(npair[0:1, 0:1], min_val=PAIRS, max_val=PAIRS + (MAX_EXTRA + 1) // 2)
                    waited = set()
                for name, k, n_dma in plan(layer):
                    s, _, _, before = units[layer][name, k]
                    if before:
                        sp.wait_ge(free(layer, s), before)
                    elif layer == 1:
                        n0, _, u0 = moe_at[0]
                        sp.wait_ge(free(0, s), n_pair * 2 + u0[s])
                    t = ring[s]
                    if name == "ln":
                        for a, w in enumerate(("ln1_g", "ln1_b", "ln2_g", "ln2_b")):
                            sp.dma_start(t[32 * a:32 * a + 32, 0:P], i[w].rearrange("l (c p) -> (l c) p", p=P))\
                              .then_inc(full(layer, s), 16)
                        sp.dma_start(lay[0].S[0:96, 0:L1], i["alibi"]).then_inc(full(layer, s), 16)
                    elif name == "x" or name == "mem":
                        x = i["x_prompt" if name == "x" else "mem_prompt"][0]
                        sp.dma_start(t[:, :].rearrange("p (a d) -> p a d", a=2),
                                     x.rearrange("(a p) d -> p a d", p=P)).then_inc(full(layer, s), 16)
                    elif name == "xs":
                        sp.dma_start(t[0:NB, 0:D], i["x_sample"].rearrange("b a d -> (b a) d"))\
                          .then_inc(full(layer, s), 16)
                    elif name == "kiwi":
                        c0 = QI_AT + IH * 64
                        wload(layer, s, win, None, c0, 64, 0, 144)
                        wload(layer, s, win, None, c0, 80, 64, 144)
                    elif name == "f":
                        wload(layer, s, win, None, H * P + 2 * W, H)
                    elif name in ("qi", "q", "kv", "qm"):
                        c0 = {"qi": QI_AT, "q": 0, "kv": col_kv, "qm": col_qm}[name]
                        wload(layer, s, win, k % 2, c0 + 512 * (k // 2), 512)
                    elif name == "mkv":
                        wload(layer, s, i["w_mem_kv"][layer], k % 2, 512 * (k // 2), 512)
                    elif name == "o":
                        wload(layer, s, i["w_o"][layer], k % 2, 512 * (k // 2), 512)
                    elif name == "ik":
                        for b in range(4 * k, 4 * k + 4):
                            pages(layer, s, b, 0, PAGES, i["cache_a_ik"][0],
                                  lambda g: t[:, ((b % 4) * PAGES + g) * 64:((b % 4) * PAGES + g + 1) * 64])
                    elif name == "lf":
                        for b in range(NB):
                            pages(layer, s, b, 0, PAGES, i["cache_b_lf"][0],
                                  lambda g: t[:, g * 96 + b * H:g * 96 + (b + 1) * H])
                    elif name in ("k", "v"):
                        per = UNIT // W
                        b, first = divmod(k * per, PAGES)
                        pages(layer, s, b, first, per, ck if name == "k" else cv,
                              lambda g: t[:, (g - first) * W:(g - first + 1) * W])
                    elif name in ("mk", "mv"):
                        c = i["cache_mem_k" if name == "mk" else "cache_mem_v"][layer]
                        for b in range(4):
                            sp.dma_start(t[:, b * 1024:(b + 1) * 1024].rearrange("p (a w) -> p a w", a=2),
                                         c[4 * k + b].rearrange("(a p) h d -> p a (h d)", p=P))\
                              .then_inc(full(layer, s), 16)
                    elif name == "r":
                        sp.dma_start(t[0:16, 0:512], i["w_r1"][layer].rearrange("(c p) j -> c (p j)", p=P))\
                          .then_inc(full(layer, s), 16)
                        for g in range(4):
                            sp.dma_start(t[16 + 16 * g:32 + 16 * g, 0:512],
                                         i["w_r2"][layer, g].rearrange("(c p) j -> c (p j)", p=P))\
                              .then_inc(full(layer, s), 16)
                wg, wu, wd = (i[n][layer] for n in ("w_gate", "w_up", "w_down"))

                def pass_loads(it, experts, reuse):
                    for k in range(12):
                        s, _, freed = moe_unit(layer, k, it)
                        sp.wait_ge(free(layer, s), freed - 1)
                        e = experts[k // 4 if k < 8 else (k - 8) // 2]
                        half = k % 2
                        if k < 8:
                            w = (wg if k % 4 < 2 else wu)[bass.ds(e, 1)]
                            src = w.rearrange("a (c p) f -> p (a c) f", p=P)[:, 8 * half:8 * half + 8, :]
                            dst = ring[s][:, :].rearrange("p (c f) -> p c f", f=FE)
                        else:
                            src = wd[bass.ds(e, 1)].rearrange("a (c p) f -> p (a c) f", p=P)[:, 2 * half:2 * half + 2, :]
                            dst = ring[s][:, :].rearrange("p (c f) -> p c f", f=D)
                        sp.dma_start(dst, src).then_inc(full(layer, s), 16)

                with sp.Fori(0, PAIRS) as it:
                    pass_loads(it, (it * 2, it * 2 + 1), True)
                sp.wait_ge(S(f"route_done_l{layer}"), 1)
                n_all = sp.value_load(npair[0:1, 0:1], min_val=PAIRS, max_val=PAIRS + (MAX_EXTRA + 1) // 2)
                with sp.If(n_all > PAIRS):
                    with sp.Fori(PAIRS, n_all) as it:
                        sp.reg_load(pregs[0:2], ent[0:1, bass.ds(it * 2, 2)])
                        experts = [sp.snap(g, min_val=0, max_val=NE - 1) for g in pregs[0:2]]
                        pass_loads(it, experts, True)
            sp.wait_ge(S("stored"), 16 * N_STORES)

        @block.gpsimd
        def _(pool):
            for layer in range(2):
                a = lay[layer]
                if layer == 0:
                    pool.memset(a.QIz, 0.0).then_inc(S("zeroed"), 1)
                pool.wait_ge(S("memory_done"), layer + 1)
                pool.memset(a.Qz[:, 0:a.nk * NB * 96], 0.0).then_inc(S("zeroed"), 1)
                pool.memset(a.Qmz, 0.0).then_inc(S("zeroed"), 1)
                pool.wait_ge(S("mixed"), 16 * (2 * layer + 1))
                pool.memset(AT[:, :], 0.0).then_inc(S("zeroed"), 1)
                pool.memset(M.lg, 0.0).then_inc(S("zeroed"), 1)
                pool.memset(M.ys, 0.0).then_inc(S(f"rows_out_l{layer}"), 1)
                pool.memset(M.gt, 0.0).then_inc(S(f"gt_copied_l{layer}"), 1)
        ZERO = [1, 3, 5, 7, 9]

        @block.tensor
        def _(pe):
            cnt = {}

            def bump(name, k=1):
                cnt[name] = cnt.get(name, 0) + k
                return cnt[name]

            pe.wait_ge(S("consts_in"), 16)

            def turn_rows(layer, name):
                t = arrived(pe, layer, name)
                if name == "x":
                    ts = arrived(pe, layer, "xs")
                for c in range(KC):
                    n = bump("rows_turned")
                    if n > 4:
                        pe.wait_ge(S("rows_copied"), n - 4)
                    b = B[n % 4]
                    for g in range(2):
                        mm = pe.transpose(b[:, g * P:(g + 1) * P], t[:, g * D + c * P:g * D + (c + 1) * P], ident)
                    if name == "x":
                        mm = pe.transpose(b[:, SEQ:T], ts[0:NB, c * P:(c + 1) * P], ident[0:NB, 0:NB])
                    mm.then_inc(S("rows_turned"), 1)
                pe.wait_ge(S("rows_copied"), n)
                mm = pe.transpose(B[4][:, 0:P], ident, ident)
                leave(mm, layer, name)
                if name == "x":
                    mm = pe.transpose(B[4][:, 0:P], ident, ident)
                    leave(mm, layer, "xs")

            def slab(layer, name, k, src, n_tok):
                g = bump("slab")
                if g > 2:
                    pe.wait_ge(S("slab_copied"), g - 2)
                for half in range(2):
                    u = arrived(pe, layer, name, 2 * k + half)
                    for f in range(4):
                        for c in range(8):
                            mm = pe.matmul(B[4 * (g % 2) + f][:, 0:n_tok],
                                           u[:, c * 512 + f * P:c * 512 + (f + 1) * P],
                                           src[8 * half + c][:, 0:n_tok],
                                           start=(half == 0 and c == 0), stop=(half == 1 and c == 7))
                    leave(mm, layer, name, 2 * k + half)

            def slabs_done():
                pe.wait_ge(S("slab_copied"), cnt["slab"])

            def natural(src, nh, n_items, col=T):
                for t in range(n_items):
                    n = bump("natural")
                    if n > 2:
                        pe.wait_ge(S("natural_copied"), n - 2)
                    rows = P if t < 2 else NB
                    for h in range(nh):
                        mm = pe.transpose(B[4 + n % 2][0:rows, h * P:(h + 1) * P],
                                          src[:, h * col + t * P:h * col + t * P + rows], ident)
                    mm.then_inc(S("natural_ready"), 1)

            def memory(layer, a):
                slabs_done()
                turn_rows(layer, "mem")
                for k in range(2):
                    slab(layer, "mkv", k, Ac, SEQ)
                slabs_done()
                natural(a.memK, HM, 2, SEQ)
                natural(a.mvT, HM, 2, SEQ)
                pe.wait_ge(S("natural_copied"), cnt["natural"])

            def indexer(a):
                u = arrived(pe, 0, "kiwi")
                for c in range(KC):
                    pe.matmul(B[4][:, 0:T], u[:, c * 144:c * 144 + P], Xc[c], start=(c == 0), stop=(c == KC - 1))
                for c in range(KC):
                    mm = pe.matmul(B[5][0:IH, 0:T], u[:, c * 144 + P:c * 144 + 144], Xc[c],
                                   start=(c == 0), stop=(c == KC - 1))
                leave(mm, 0, "kiwi")
                pe.wait_ge(S("kiwi_copied"), 2)
                for t in range(2):
                    pe.transpose(B[6][:, 64 * t:64 * t + 64], a.KI[0:64, t * P:(t + 1) * P], ident[0:64, 0:64])
                    pe.transpose(B[6][:, 192 + IH * t:192 + IH * (t + 1)], a.WI[:, t * P:(t + 1) * P],
                                 ident[0:IH, 0:IH])
                pe.transpose(B[6][0:NB, P:P + 64], a.KI[0:64, SEQ:T], ident[0:64, 0:64]).then_inc(S("kiwi_rows"), 1)
                pe.matmul(B[7][:, 0:NB], cst("rep16", IH), a.WI[:, SEQ:T], start=True, stop=True)\
                  .then_inc(S("wblock"), 1)
                pe.wait_ge(S("kiwi_rows_copied"), 3)
                pe.wait_ge(S("wblock_copied"), 1)
                for k in range(2):
                    slab(0, "qi", k, Xc, T)
                slabs_done()
                for n in range(16):
                    t, c = divmod(n, 8)
                    if n >= 2:
                        pe.wait_ge(S("ixp_relu"), n - 1)
                    for s in range(2):
                        mm = pe.matmul(B[4 + 2 * (n % 2) + s][:, 0:SEQ],
                                       a.qiT[64 * s:64 * s + 64, c * T + t * P:c * T + (t + 1) * P],
                                       a.KI[64 * s:64 * s + 64, 0:SEQ], start=True, stop=True)
                    mm.then_inc(S("ixp_scores"), 1)
                pe.wait_ge(S("qiz_built"), 2)
                pe.wait_ge(S("ixp_relu"), 16)
                us = [arrived(pe, 0, "ik", k) for k in range(2)]

                def product(n):
                    j, b = divmod(n, NB)
                    pe.wait_ge(S("kt_copied"), n + 1)
                    if b == 0 and j >= 2:
                        pe.wait_ge(S("ix_relu"), j - 1)
                    mm = pe.matmul(B[2 + j % 2][:, :], a.QIz[:, b * P:(b + 1) * P],
                                   a.KTs[:, 512 * (n % 2):512 * (n % 2) + 512], start=(b == 0), stop=(b == NB - 1))
                    if b == NB - 1:
                        mm.then_inc(S("ix_scores"), 1)

                def rows(j):
                    w = 512 if j < 4 else 1
                    pe.wait_ge(S("ix_relu"), j + 1)
                    if j:
                        pe.wait_ge(S("ix_rows_copied"), j)
                    pe.matmul(B[5][96:96 + NB, 0:w], a.Wb, a.tb[:, 0:w], start=True, stop=True)\
                      .then_inc(S("ix_rows"), 1)

                for n in range(32):
                    j, b = divmod(n, NB)
                    bump("kt")
                    if n >= 2:
                        pe.wait_ge(S("kt_copied"), n - 1)
                    for pg in range(4):
                        at = ((b % 4) * PAGES + 4 * j + pg) * 64
                        for s in range(2):
                            mm = pe.matmul(B[n % 2][64 * s:64 * s + 64, pg * P:(pg + 1) * P],
                                           us[b // 4][:, at:at + 64], ident, start=True, stop=True)
                    mm.then_inc(S("kt_ready"), 1)
                    if n:
                        product(n - 1)
                        if n % NB == 1 and n > NB:
                            rows(j - 1)
                product(31)
                for b in range(NB):
                    if b == 0:
                        pe.wait_ge(S("ixp_relu"), 16)
                    mm = pe.matmul(B[4][:, 0:1], a.QIz[:, b * P:(b + 1) * P], a.KI[:, SEQ + b:SEQ + b + 1],
                                   start=(b == 0), stop=(b == NB - 1))
                    if b in (0, 1):
                        leave(mm, 0, "ik", b)
                mm.then_inc(S("ix_scores"), 1)
                rows(3)
                rows(4)
                pe.wait_ge(S("ix_rows_copied"), 5)

            def forget_gates(a):
                u = arrived(pe, 1, "f")
                for c in range(KC):
                    mm = pe.matmul(B[4][0:H, 0:T], u[:, c * H:(c + 1) * H], Xc[c], start=(c == 0), stop=(c == KC - 1))
                leave(mm, 1, "f")
                pe.wait_ge(S("lf_ready"), 2)
                for t in range(3):
                    rows = P if t < 2 else NB
                    pe.transpose(B[5][0:rows, t * H:(t + 1) * H], a.fx[:, t * P:t * P + rows], ident[0:H, 0:H])
                for t in range(2):
                    mm = pe.transpose(B[5][:, (3 + t) * H:(4 + t) * H], a.fe[:, t * P:(t + 1) * P], ident[0:H, 0:H])
                pe.matmul(B[6][0:96, 0:8], cst("rep12", H), a.fx[:, SEQ:T], start=True, stop=True)\
                  .then_inc(S("lf_rows"), 1)
                pe.wait_ge(S("lf_nat"), 3)
                pe.wait_ge(S("lf_rows_copied"), 1)

            def cached_gates(a):
                pe.wait_ge(S("natural_copied"), cnt["natural"])
                u = arrived(pe, 1, "lf")
                for j in range(4):
                    for pg in range(4):
                        mm = pe.transpose(B[j][0:96, pg * P:(pg + 1) * P], u[:, (4 * j + pg) * 96:(4 * j + pg + 1) * 96],
                                          ident)
                    mm.then_inc(S("lf_turned"), 1)
                pe.wait_ge(S("lf_copied"), 4)
                leave(pe.transpose(B[4][:, 0:P], ident, ident), 1, "lf")

            def sample_scores(layer, a):
                pe.wait_ge(S("qz_built"), (a.nk + 1) * (layer + 1) if layer == 0 else (2 + 1) + (4 + 1))
                per = UNIT // a.W
                steps = []
                for u in range(NB * PAGES // per):
                    b, first = divmod(u * per, PAGES)
                    for kv in range(a.nk):
                        for j in range(first // 4, (first + per) // 4):
                            steps.append((u, b, kv, j, first))
                pending = []

                def product(st, n):
                    u, b, kv, j, first = st
                    pe.wait_ge(S("kt_copied"), n)
                    return pe.matmul(B[j][0:96, :], a.Qz[:, (kv * NB + b) * 96:(kv * NB + b + 1) * 96],
                                     a.KTs[:, 512 * (n % 2):512 * (n % 2) + 512],
                                     start=(b == 0 and kv == 0), stop=(b == NB - 1 and kv == a.nk - 1))

                last = None
                for k, st in enumerate(steps):
                    u, b, kv, j, first = st
                    tile = arrived(pe, layer, "k", u) if (k == 0 or steps[k - 1][0] != u) else ring[units[layer]["k", u][0]]
                    n = bump("kt")
                    if n > 2:
                        pe.wait_ge(S("kt_copied"), n - 2)
                    for pg in range(4):
                        at = (4 * j + pg - first) * a.W + kv * P
                        mm = pe.transpose(B[4 + n % 2][:, pg * P:(pg + 1) * P], tile[:, at:at + P], ident)
                    mm.then_inc(S("kt_ready"), 1)
                    if last is not None:
                        mm = product(last, n - 1)
                        if k + 1 == len(steps) or steps[k + 1][0] != u:
                            leave(mm, layer, "k", u)
                    last = st
                product(last, n)
                for b in range(NB):
                    for kv in range(a.nk):
                        mm = pe.matmul(B[6][0:96, 0:1], a.Qz[:, (kv * NB + b) * 96:(kv * NB + b + 1) * 96],
                                       a.kT[:, kv * T + SEQ + b:kv * T + SEQ + b + 1],
                                       start=(b == 0 and kv == 0), stop=(b == NB - 1 and kv == a.nk - 1))
                mm.then_inc(S("k_scores"), 1)

                def mem_product(b, hp, n):
                    pe.wait_ge(S("kt_copied"), n)
                    for s in range(2):
                        h = 2 * hp + s
                        mm = pe.matmul(B[7][0:32, 0:SEQ], a.Qmz[:, (h * NB + b) * 32:(h * NB + b + 1) * 32],
                                       a.KTs[:, 512 * (n % 2) + SEQ * s:512 * (n % 2) + SEQ * (s + 1)],
                                       start=(b == 0 and h == 0), stop=(b == NB - 1 and h == HM - 1))
                    return mm

                last = None
                for b in range(NB):
                    tile = arrived(pe, layer, "mk", b // 4) if b % 4 == 0 else ring[units[layer]["mk", b // 4][0]]
                    for hp in range(2):
                        n = bump("kt")
                        pe.wait_ge(S("kt_copied"), n - 2)
                        for s in range(2):
                            for pg in range(2):
                                at = ((b % 4) * 2 + pg) * 512 + (2 * hp + s) * P
                                mm = pe.transpose(B[4 + n % 2][:, (2 * s + pg) * P:(2 * s + pg + 1) * P],
                                                  tile[:, at:at + P], ident)
                        mm.then_inc(S("kt_ready"), 1)
                        if last is not None:
                            mm = mem_product(*last, n - 1)
                            if b % 4 == 3 and hp == 1:
                                leave(mm, layer, "mk", b // 4)
                        last = (b, hp)
                mem_product(*last, n).then_inc(S("km_scores"), 1)
                pe.wait_ge(S("scores_added"), layer + 1)

            def prompt_attention(layer, a):
                base = 16 * layer
                items = [("self", t, hp) for t in range(2) for hp in range(6)] + \
                        [("mem", t, hp) for t in range(2) for hp in range(2)]
                for n in range(len(items) + 2):
                    if n < len(items):
                        kind, t, hp = items[n]
                        if n >= 2:
                            pe.wait_ge(S("p_max"), base + n - 1)
                        for s in range(2):
                            h = 2 * hp + s
                            out = B[n % 2][:, s * SEQ:(s + 1) * SEQ]
                            if kind == "self":
                                kv = h // a.G
                                mm = pe.matmul(out, a.qT[:, h * T + t * P:h * T + (t + 1) * P],
                                               a.kT[:, kv * T:kv * T + SEQ], start=True, stop=(layer == 0))
                                if layer == 1:
                                    mm = pe.matmul(out, ident[0:H, h:h + 1].broadcast_to((H, P)), a.fe[:, 0:SEQ],
                                                   start=False, stop=True)
                            else:
                                mm = pe.matmul(out, a.qmT[:, h * T + t * P:h * T + (t + 1) * P],
                                               a.memK[:, h * SEQ:(h + 1) * SEQ], start=True, stop=True)
                        mm.then_inc(S("p_scores"), 1)
                    if 1 <= n <= len(items):
                        m = n - 1
                        pe.wait_ge(S("p_norm"), base + m + 1)
                        if m >= 2:
                            pe.wait_ge(S("p_turned_copied"), base + m - 1)
                        for k in range(4):
                            mm = pe.transpose(B[2 + m % 2][:, k * P:(k + 1) * P], a.sc[m % 2][:, k * P:(k + 1) * P], ident)
                        mm.then_inc(S("p_turned"), 1)
                    if n >= 2:
                        m = n - 2
                        kind, t, hp = items[m]
                        pe.wait_ge(S("p_turned_copied"), base + m + 1)
                        if m >= 2:
                            pe.wait_ge(S("p_out_copied"), base + m - 1)
                        for s in range(2):
                            h = 2 * hp + s
                            for g in range(2):
                                v = a.VN[:, g * a.W + (h // a.G) * P:g * a.W + (h // a.G + 1) * P] if kind == "self" \
                                    else a.memV[:, g * 512 + h * P:g * 512 + (h + 1) * P]
                                mm = pe.matmul(B[4 + m % 2][:, s * P:(s + 1) * P], v,
                                               a.PTp[m % 2][:, (2 * s + g) * P:(2 * s + g + 1) * P],
                                               start=(g == 0), stop=(g == 1))
                        mm.then_inc(S("p_out"), 1)
                pe.wait_ge(S("p_out_copied"), base + len(items))

            def sample_attention(layer, a):
                if layer == 0:
                    pe.wait_ge(S("mask_ready"), 1)
                    for j in range(4):
                        pe.matmul(B[j][0:96, :], cst("to12", NB, 96), a.S[96:96 + NB, 512 * j:512 * j + 512],
                                  start=True, stop=True)
                    pe.matmul(B[4][0:96, 0:1], cst("to12", NB, 96), a.S[96:96 + NB, PAST:L1], start=True, stop=True)\
                      .then_inc(S("mask_rows"), 1)
                pe.wait_ge(S("s_norm"), layer + 1)
                for pg in range(PAGES):
                    mm = pe.transpose(B[pg // 5][:, (pg % 5) * 96:(pg % 5 + 1) * 96], a.S[0:96, pg * P:(pg + 1) * P],
                                      ident[0:96, 0:96])
                pe.transpose(B[4][0:NB, 0:96], a.epn, ident[0:96, 0:96])
                for g in range(2):
                    mm = pe.transpose(B[5][:, 32 * g:32 * g + 32], a.Sm[:, g * P:(g + 1) * P], ident[0:32, 0:32])
                mm.then_inc(S("s_turned"), 1)
                pe.wait_ge(S("s_turned_copied"), 6 * (layer + 1))
                per = UNIT // a.W

                def turn_out(b):
                    pe.wait_ge(S("ov_copied"), 16 * layer + b + 1)
                    for kv in range(a.nk):
                        at = (b * a.nk + kv) * H
                        mm = pe.transpose(B[5][:, at:at + H], a.ovs[0:H, kv * P:(kv + 1) * P], ident[0:H, 0:H])
                    mm.then_inc(S("ov_turned"), 1)

                for b in range(NB):
                    out = B[6 + b % 2][0:H, 0:a.W]
                    if b >= 2:
                        pe.wait_ge(S("ov_copied"), 16 * layer + b - 1)
                    for u in range(b * PAGES // per, (b + 1) * PAGES // per):
                        tile = arrived(pe, layer, "v", u)
                        for k in range(per):
                            pg = (u * per) % PAGES + k
                            mm = pe.matmul(out, a.PT[:, pg * 96 + b * H:pg * 96 + (b + 1) * H],
                                           tile[:, k * a.W:(k + 1) * a.W], start=(pg == 0), stop=False)
                        leave(mm, layer, "v", u)
                    pe.matmul(out, a.PTn[:, b * H:(b + 1) * H], a.VNs, start=False, stop=True).then_inc(S("ov_ready"), 1)
                    if b:
                        turn_out(b - 1)
                turn_out(NB - 1)

                def turn_mem(b):
                    pe.wait_ge(S("ov_copied"), 16 * layer + NB + b + 1)
                    for h in range(HM):
                        at = (b * HM + h) * 4
                        mm = pe.transpose(B[4][:, at:at + 4], a.ovs[0:4, h * P:(h + 1) * P], ident[0:4, 0:4])
                    mm.then_inc(S("ov_turned"), 1)

                for b in range(NB):
                    out = B[6 + b % 2][0:4, :]
                    pe.wait_ge(S("ov_copied"), 16 * layer + NB + b - 1)
                    tile = arrived(pe, layer, "mv", b // 4) if b % 4 == 0 else ring[units[layer]["mv", b // 4][0]]
                    for g in range(2):
                        mm = pe.matmul(out, a.PTm[:, 32 * g + 4 * b:32 * g + 4 * b + 4],
                                       tile[:, ((b % 4) * 2 + g) * 512:((b % 4) * 2 + g + 1) * 512],
                                       start=(g == 0), stop=(g == 1))
                    mm.then_inc(S("ov_ready"), 1)
                    if b:
                        turn_mem(b - 1)
                turn_mem(NB - 1)
                for k in range(2):
                    leave(pe.transpose(B[7][:, 0:P], ident, ident), layer, "mv", k)
                pe.wait_ge(S("at_done"), layer + 1)

            def layer_norm(k):
                for c in range(KC):
                    pe.wait_ge(S("mixed"), 16 * k + max(c + 1, 12))
                    mm = pe.matmul(B[0][:, 0:T], cst("mean"), Xc[c], start=(c == 0), stop=(c == KC - 1))
                mm.then_inc(S("ln_mean"), 1)
                for c in range(KC):
                    pe.wait_ge(S("ln_square"), 16 * k + c + 1)
                    pe.matmul(B[1][:, 0:T], cst("mean"), M.sq[c % 2], start=(c == 0), stop=(c == KC - 1))\
                      .then_inc(S("ln_square_used"), 1)
                pe.wait_ge(S("ln_out"), 16 * (k + 1))

            def router_weights(layer):
                u = arrived(pe, layer, "r")
                for j in range(4):
                    mm = pe.transpose(B[6][:, j * 80:(j + 1) * 80], u[0:80, j:j + 4 * (P - 1) + 1:4], ident[0:80, 0:80])
                leave(mm, layer, "r")

            def token_rows(k, last):
                for t in range(3):
                    rows = P if t < 2 else NB
                    for q in range(4):
                        n = bump("token_rows")
                        if n > 4:
                            pe.wait_ge(S("token_rows_copied"), n - 4)
                        for c in range(4):
                            mm = pe.transpose(B[2 + n % 4][0:rows, c * P:(c + 1) * P],
                                              Xc[4 * q + c][:, t * P:t * P + rows], ident)
                        mm.then_inc(S("token_rows"), 1)

            def experts(layer):
                sm = lambda name: S(f"{name}_l{layer}")
                pe.wait_ge(S("wr_copied"), layer + 1)
                for c in range(KC):
                    mm = pe.matmul(B[7][0:20, 0:T], wr[:, 20 * c:20 * c + 20], Xc[c], start=(c == 0), stop=(c == KC - 1))
                mm.then_inc(S("logits"), 1)
                token_rows(2 * layer, False)
                pe.wait_ge(S("logits_copied"), layer + 1)
                for t in range(3):
                    rows = P if t < 2 else NB
                    mm = pe.transpose(B[6][0:rows, 20 * t:20 * t + 20], M.lgT[:, t * P:t * P + rows], ident[0:20, 0:20])
                mm.then_inc(S("logit_rows"), 1)
                pe.wait_ge(S("chosen"), layer + 1)
                sel = M.w16[0]
                for t in range(4):
                    out = B[7][:, 16 * t:16 * t + 16]
                    for g in range(min(t + 1, 3)):
                        rows = P if g < 2 else NB
                        m = cst("before") if g == t else cst("ones")
                        mm = pe.matmul(out, m[0:rows, :], sel[0:rows, 16 * g:16 * g + 16],
                                       start=(g == 0), stop=(g == min(t, 2)))
                mm.then_inc(S("ranks"), 1)
                pe.wait_ge(S("token_rows_copied"), cnt["token_rows"])
                pe.wait_ge(S("zeroed"), ZERO[2] if layer == 0 else ZERO[4])
                pe.wait_ge(S(f"route_done_l{layer}"), 1)
                n_pair = pe.value_load(npair[0:1, 0:1], min_val=PAIRS, max_val=PAIRS + (MAX_EXTRA + 1) // 2)

                def gather(done):
                    pe.wait_ge(sm("chosen_slots"), done + 1)
                    for q in range(4):
                        if q >= 2:
                            pe.wait_ge(sm("gather_copied"), done * 4 + (q - 1))
                        for c in range(4):
                            for t in range(3):
                                rows = P if t < 2 else NB
                                mm = pe.matmul(B[6 + q % 2][:, c * P:(c + 1) * P],
                                               M.xtok[0:rows, t * D + (4 * q + c) * P:t * D + (4 * q + c + 1) * P],
                                               M.sel[0:rows, t * P:(t + 1) * P], start=(t == 0), stop=(t == 2))
                        mm.then_inc(sm("gathered"), 1)

                def scatter(it, c):
                    if c >= 2:
                        pe.wait_ge(sm("scatter_added"), it * 16 + (c - 1))
                    pe.matmul((B[2] if c % 2 == 0 else B[6])[:, 0:T], M.ys[:, c * P:(c + 1) * P], M.gt,
                              start=True, stop=True).then_inc(sm("scattered"), 1)

                def gate_up(it, s, between):
                    for k in range(4):
                        slot, v, _ = moe_unit(layer, 4 * s + k, it)
                        pe.wait_ge(full(layer, slot), v)
                        for c in range(8):
                            mm = pe.matmul(B[k // 2][64 * s:64 * s + 64, :],
                                           M.xsT[:, (8 * (k % 2) + c) * P + 64 * s:(8 * (k % 2) + c) * P + 64 * s + 64],
                                           ring[slot][:, c * FE:(c + 1) * FE],
                                           start=(k % 2 == 0 and c == 0), stop=(k % 2 == 1 and c == 7))
                            if c == 7:
                                mm.then_inc(free(layer, slot), 1)
                            between(8 * k + c)

                def turn_hidden(it, s):
                    pe.wait_ge(sm("hidden"), it * 2 + (s + 1))
                    for f in range(4):
                        mm = pe.matmul(B[3][:, 256 * s + 64 * f:256 * s + 64 * (f + 1)],
                                       M.hh[64 * s:64 * s + 64, f * P:(f + 1) * P],
                                       ident[64 * s:64 * s + 64, 64 * s:64 * s + 64], start=True, stop=True)
                    mm.then_inc(sm("hidden_turned"), 1)

                def down(it, s):
                    pe.wait_ge(sm("hidden_copied"), it * 2 + (s + 1))
                    uu = [moe_unit(layer, 8 + 2 * s + k, it) for k in range(2)]
                    for slot, v, _ in uu:
                        pe.wait_ge(full(layer, slot), v)
                    for q in range(4):
                        if q >= 2 or s == 1:
                            pe.wait_ge(sm("rows_out"), it * 8 + (4 * s + q))
                        for f in range(4):
                            mm = pe.matmul(B[4 + q % 2][64 * s:64 * s + 64, :],
                                           M.hT[:, 256 * s + 64 * f:256 * s + 64 * (f + 1)],
                                           ring[uu[f // 2][0]][:, (f % 2) * D + q * 512:(f % 2) * D + (q + 1) * 512],
                                           start=(f == 0), stop=(f == 3))
                            if q == 3 and f == 1:
                                mm.then_inc(free(layer, uu[0][0]), 1)
                        if q < 3:
                            mm.then_inc(sm("down_ready"), 1)
                        else:
                            mm.then_inc(free(layer, uu[1][0]), 1)

                gather(0)
                with pe.Fori(0, n_pair) as it:
                    pe.wait_ge(sm("gather_copied"), it * 4 + 4)
                    pe.wait_ge(sm("rows_out"), it * 8 + 1)
                    pe.wait_ge(sm("gt_copied"), it + 1)

                    def with_scatter(k):
                        if k % 2 == 1:
                            scatter(it, k // 2)

                    def with_turn(k):
                        if k == 15:
                            turn_hidden(it, 0)

                    gate_up(it, 0, with_scatter)
                    pe.wait_ge(sm("scatter_added"), it * 16 + 16)
                    for t in range(3):
                        rows = P if t < 2 else NB
                        mm = pe.transpose(B[2][:, t * P:t * P + rows], M.sg[0:rows, t * P:(t + 1) * P],
                                          ident[0:rows, 0:rows])
                    mm.then_inc(sm("gt_ready"), 1)
                    gate_up(it, 1, with_turn)
                    gather(it + 1)
                    turn_hidden(it, 1)
                    down(it, 0)
                    down(it, 1)
                pe.wait_ge(sm("rows_out"), n_pair * 8 + 1)
                pe.wait_ge(sm("gt_copied"), n_pair + 1)
                pe.wait_ge(sm("gather_copied"), n_pair * 4 + 4)
                for c in range(KC):
                    scatter(n_pair, c)

            u = None
            t = arrived(pe, 0, "ln")
            pe.transpose(B[5][:, 0:P], t[:, 0:P], ident).then_inc(free(0, units[0]["ln", 0][0]), 1)
            turn_rows(0, "x")
            for layer in range(2):
                a = lay[layer]
                if layer == 0:
                    pe.wait_ge(S("lnp_copied"), 1)
                    indexer(a)
                else:
                    forget_gates(a)
                for k in range(3):
                    slab(layer, "q", k, Xc, T)
                for k in range(1 if layer == 0 else 2):
                    slab(layer, "kv", k, Xc, T)
                slab(layer, "qm", 0, Xc, T)
                slabs_done()
                natural(a.kT, a.nk, 3)
                natural(a.vT, a.nk, 3)
                if layer == 1:
                    cached_gates(a)
                pe.wait_ge(S("natural_copied"), cnt["natural"])
                memory(layer, a)
                sample_scores(layer, a)
                prompt_attention(layer, a)
                sample_attention(layer, a)
                router_weights(layer)
                for k in range(4):
                    g = bump("mix")
                    gl = cnt["slab"]
                    for half in range(2):
                        u = arrived(pe, layer, "o", 2 * k + half)
                        if k >= 2 and half == 0:
                            pe.wait_ge(S("mixed"), 32 * layer + 4 * (k - 1))
                        bank0 = 4 * (k % 2)
                        if k == 1 and half == 0:
                            pe.wait_ge(S("wr_copied"), layer + 1)
                        for f in range(4):
                            for c in range(8):
                                mm = pe.matmul(B[bank0 + f][:, 0:T], u[:, c * 512 + f * P:c * 512 + (f + 1) * P],
                                               Ac[8 * half + c], start=(half == 0 and c == 0),
                                               stop=(half == 1 and c == 7))
                        leave(mm, layer, "o", 2 * k + half)
                layer_norm(2 * layer)
                experts(layer)
                layer_norm(2 * layer + 1)
            token_rows(4, True)

        stores = [0]

        @block.scalar
        def _(act):
            cnt = {}

            def bump(name, k=1):
                cnt[name] = cnt.get(name, 0) + k
                return cnt[name]

            def copy(out, in_, scale=1.0):
                return act.activation(out, in_, ACT.Copy, scale=scale)

            def store(dst, src):
                stores[0] += 1
                act.dma_start(dst, src).then_inc(S("stored"), 16)

            def turn_rows(dst, n_tok):
                for c in range(KC):
                    n = bump("rows")
                    act.wait_ge(S("rows_turned"), n)
                    copy(dst[c][:, 0:n_tok], B[n % 4][:, 0:n_tok]).then_inc(S("rows_copied"), 1)

            def slab(layer, name, k, dsts, n_tok, scale=1.0):
                g = bump("slab")
                left(act, layer, name, 2 * k + 1)
                for f in range(4):
                    c = copy(dsts[f], B[4 * (g % 2) + f][:, 0:n_tok], scale)
                c.then_inc(S("slab_copied"), 1)

            def natural(dsts, w):
                for rows, dst in dsts:
                    n = bump("natural")
                    act.wait_ge(S("natural_ready"), n)
                    copy(dst, B[4 + n % 2][0:rows, 0:w]).then_inc(S("natural_copied"), 1)

            def heads(t, n, w=T):
                return [t[:, k * w:(k + 1) * w] for k in range(n)]

            def indexer(a):
                left(act, 0, "kiwi")
                copy(a.KI, B[4][:, 0:T]).then_inc(S("kiwi_copied"), 1)
                copy(a.WI, B[5][0:IH, 0:T], IH ** -0.5).then_inc(S("kiwi_copied"), 1)
                act.wait_ge(S("kiwi_rows"), 1)
                copy(a.nat[:, 0:P], B[6][:, 0:P]).then_inc(S("kiwi_rows_copied"), 1)
                copy(a.nat[0:NB, P:192], B[6][0:NB, P:192]).then_inc(S("kiwi_rows_copied"), 1)
                copy(a.nat[:, 192:224], B[6][:, 192:224]).then_inc(S("kiwi_rows_copied"), 1)
                act.wait_ge(S("kiwi_rows_copied"), 3)
                store(o["a_ik_p"][0, 0].rearrange("(t p) d -> p t d", p=P),
                      a.nat[:, 0:P].rearrange("p (t d) -> p t d", t=2))
                store(o["a_ik_s"][0].rearrange("b a d -> (b a) d"), a.nat[0:NB, P:192])
                for k in range(2):
                    slab(0, "qi", k, heads(a.qiT[:, k * 4 * T:(k + 1) * 4 * T], 4), T)
                act.wait_ge(S("zeroed"), ZERO[0])
                act.wait_ge(S("slab_copied"), 2)
                q = a.qiT[:, 0:8 * T].rearrange("p (c t) -> p c t", t=T)[:, :, SEQ:T]
                for s in range(2):
                    dst = diagonal(a.QIz, s, 64 * s, 64, [(2, 8), (P + IH, NB)])
                    copy(dst, q[64 * s:64 * s + 64]).then_inc(S("qiz_built"), 1)
                for n in range(16):
                    act.wait_ge(S("ixp_scores"), n + 1)
                    if n >= 2:
                        act.wait_ge(S("ixp_added"), n - 1)
                    for s in range(2):
                        r = act.activation(a.RL[:, 512 * (n % 2) + SEQ * s:512 * (n % 2) + SEQ * (s + 1)],
                                           B[4 + 2 * (n % 2) + s][:, 0:SEQ], ACT.Relu, scale=64 ** -0.5)
                    r.then_inc(S("ixp_relu"), 1)

                def relu(j):
                    w = 512 if j < 4 else 1
                    act.wait_ge(S("ix_scores"), j + 1)
                    if j:
                        act.wait_ge(S("ix_rows"), j)
                    act.activation(a.tb[:, 0:w], (B[2 + j % 2] if j < 4 else B[4])[:, 0:w], ACT.Relu,
                                   scale=64 ** -0.5).then_inc(S("ix_relu"), 1)

                def rows(j):
                    w = 512 if j < 4 else 1
                    act.wait_ge(S("ix_rows"), j + 1)
                    copy(a.S[96:96 + NB, 512 * j:512 * j + w], B[5][96:96 + NB, 0:w]).then_inc(S("ix_rows_copied"), 1)

                for n in range(32):
                    bump("kt")
                    act.wait_ge(S("kt_ready"), n + 1)
                    if n >= 2 and n % NB != 1:
                        pass
                    copy(a.KTs[:, 512 * (n % 2):512 * (n % 2) + 512], B[n % 2][:, :]).then_inc(S("kt_copied"), 1)
                    if n % NB == 0 and n:
                        relu(n // NB - 1)
                    if n % NB == 1 and n > 1:
                        rows(n // NB - 1)
                relu(3)
                rows(3)
                relu(4)
                rows(4)

            def diagonal(tile, offset, p0, rows, dims):
                base = tile[p0:p0 + rows, offset:offset + 1]
                v = base.copy()
                return bass.AP(tensor=v.tensor, offset=v.offset, ap=[list(v.ap[0])] + [[s, n] for s, n in dims])

            def forget_gates(a):
                left(act, 1, "f")
                act.wait_ge(S("bias_in"), 80)
                act.activation(a.fx, B[4][0:H, 0:T], ACT.Identity, bias=fbias[:, 0:1]).then_inc(S("f_biased"), 1)
                act.wait_ge(S("f_abs"), 1)
                act.activation(a.fe, a.fe, ACT.Exp, scale=-1.0).then_inc(S("f_exp"), 1)
                act.wait_ge(S("f_exp"), 1)
                act.activation(a.fe, a.fe, ACT.Ln, bias=1.0).then_inc(S("f_ln"), 1)
                act.wait_ge(S("lf_rows"), 1)
                copy(a.lfn[:, 0:2 * H], B[5][:, 0:2 * H]).then_inc(S("lf_nat"), 1)
                copy(a.lfn[0:NB, 2 * H:3 * H], B[5][0:NB, 2 * H:3 * H]).then_inc(S("lf_nat"), 1)
                copy(a.cq, B[5][:, 3 * H:5 * H], -1.0).then_inc(S("lf_nat"), 1)
                act.wait_ge(S("lf_nat"), 3)
                store(o["b_lf_p"][0, 0].rearrange("(t p) d -> p t d", p=P),
                      a.lfn[:, 0:2 * H].rearrange("p (t d) -> p t d", t=2))
                store(o["b_lf_s"][0].rearrange("b a d -> (b a) d"), a.lfn[0:NB, 2 * H:3 * H])

            def pad_queries(layer, a):
                act.wait_ge(S("zeroed"), ZERO[1] if layer == 0 else ZERO[3])
                act.wait_ge(S("slab_copied"), cnt["slab"])
                for kv in range(a.nk):
                    src = a.qT[:, :].rearrange("p (h t) -> p h t", t=T)[:, kv * a.G:(kv + 1) * a.G, SEQ:T]
                    copy(diagonal(a.Qz, kv * NB * 96 + a.G * kv, 0, P, [(1, a.G), (96 + H, NB)]), src)\
                        .then_inc(S("qz_built"), 1)
                src = a.qmT[:, :].rearrange("p (h t) -> p h t", t=T)[:, :, SEQ:T]
                copy(diagonal(a.Qmz, 0, 0, P, [(NB * 32 + 1, HM), (32 + 4, NB)]), src).then_inc(S("qz_built"), 1)

            def sample_scores(layer, a):
                steps = NB * a.nk * 4 + 2 * NB
                for _ in range(steps):
                    n = bump("kt")
                    act.wait_ge(S("kt_ready"), n)
                    copy(a.KTs[:, 512 * (n % 2):512 * (n % 2) + 512], B[4 + n % 2][:, :]).then_inc(S("kt_copied"), 1)

            def prompt_attention(layer, a):
                base = 16 * layer
                items = [("self", t, hp) for t in range(2) for hp in range(6)] + \
                        [("mem", t, hp) for t in range(2) for hp in range(2)]
                nm, rs = a.st[:, 0:4], a.st[:, 4:8]
                for n in range(len(items) + 2):
                    if n < len(items):
                        act.wait_ge(S("p_max"), base + n + 1)
                        for s in range(2):
                            x = a.sc[n % 2][:, SEQ * s:SEQ * (s + 1)]
                            k = 2 * (n % 2) + s
                            e = act.activation(x, x, ACT.Exp, bias=nm[:, k:k + 1], accum_out=rs[:, k:k + 1])
                        e.then_inc(S("p_exp"), 1)
                    if 1 <= n <= len(items):
                        m = n - 1
                        act.wait_ge(S("p_turned"), base + m + 1)
                        if m >= 2:
                            act.wait_ge(S("p_out"), base + m - 1)
                        copy(a.PTp[m % 2], B[2 + m % 2][:, :]).then_inc(S("p_turned_copied"), 1)
                    if n >= 2:
                        m = n - 2
                        kind, t, hp = items[m]
                        h = 2 * hp + (0 if kind == "self" else H)
                        act.wait_ge(S("p_out"), base + m + 1)
                        copy(Av[:, h:h + 2, t * P:(t + 1) * P],
                             B[4 + m % 2][:, 0:SEQ].rearrange("p (h t) -> p h t", h=2)).then_inc(S("p_out_copied"), 1)

            def sample_attention(layer, a):
                nm, rs = a.st[:, 8:10], a.st[:, 10:12]
                act.wait_ge(S("s_max"), layer + 1)
                act.activation(a.S[0:96, 0:L1], a.S[0:96, 0:L1], ACT.Exp, bias=nm[0:96, 0:1],
                               accum_out=rs[0:96, 0:1])
                act.activation(a.Sm, a.Sm, ACT.Exp, bias=nm[0:32, 1:2], accum_out=rs[0:32, 1:2])\
                   .then_inc(S("s_exp"), 1)
                act.wait_ge(S("s_turned"), layer + 1)
                for k in range(4):
                    w = 480 if k < 3 else 96
                    copy(a.PT[:, 480 * k:480 * k + w], B[k][:, 0:w]).then_inc(S("s_turned_copied"), 1)
                copy(a.PTn, B[4][0:NB, 0:96]).then_inc(S("s_turned_copied"), 1)
                copy(a.PTm, B[5][:, 0:64]).then_inc(S("s_turned_copied"), 1)
                for b in range(2 * NB):
                    act.wait_ge(S("ov_ready"), 16 * layer + b + 1)
                    if b:
                        act.wait_ge(S("ov_turned"), 16 * layer + b)
                    rows, w = (H, a.W) if b < NB else (4, 512)
                    copy(a.ovs[0:rows, 0:w], B[6 + b % 2][0:rows, 0:w]).then_inc(S("ov_copied"), 1)
                act.wait_ge(S("ov_turned"), 16 * layer + 16)
                for kv in range(a.nk):
                    src = B[5][:, 0:NB * a.nk * H].rearrange("p (b k h) -> p k h b", k=a.nk, h=H)
                    copy(Av[:, kv * a.G:(kv + 1) * a.G, SEQ:T], src[:, kv, kv * a.G:(kv + 1) * a.G, :])
                src = diagonal(B[4], 0, 0, P, [(5, HM), (16, NB)])
                copy(Av[:, H:H + HM, SEQ:T], src).then_inc(S("at_done"), 1)

            def layer_norm(k):
                layer, j = divmod(k, 2)
                for c in range(KC):
                    act.wait_ge(S("ln_centred"), 16 * k + c + 1)
                    if 16 * k + c >= 2:
                        act.wait_ge(S("ln_square_used"), 16 * k + c - 1)
                    act.activation(M.sq[c % 2], Xc[c], ACT.Square).then_inc(S("ln_square"), 1)
                act.wait_ge(S("ln_var"), k + 1)
                act.activation(M.rstd, M.rstd, ACT.Sqrt).then_inc(S("ln_std"), 1)
                for c in range(KC):
                    act.wait_ge(S("ln_normed"), 16 * k + c + 1)
                    g = 64 * j + 16 * layer + c
                    act.activation(Xc[c], Xc[c], ACT.Identity, bias=lnp[:, g + 32:g + 33], scale=lnp[:, g:g + 1])\
                       .then_inc(S("ln_out"), 1)

            def token_rows(last):
                for t in range(3):
                    rows = P if t < 2 else NB
                    for q in range(4):
                        n = bump("token_rows")
                        act.wait_ge(S("token_rows"), n)
                        copy(M.xtok[0:rows, t * D + 512 * q:t * D + 512 * (q + 1)], B[2 + n % 4][0:rows, :])\
                            .then_inc(S("token_rows_copied"), 1)
                    if last:
                        act.wait_ge(S("token_rows_copied"), n)
                        dst = o["y_prompt"][0, t * P:(t + 1) * P, :] if t < 2 else o["y_sample"].rearrange("b a d -> (b a) d")
                        store(dst, M.xtok[0:rows, t * D:(t + 1) * D])

            def experts(layer):
                sm = lambda name: S(f"{name}_l{layer}")
                act.wait_ge(S("bias_in"), 80)
                act.wait_ge(S("logits"), layer + 1)
                act.activation(M.lgT, B[7][0:20, 0:T], ACT.Identity, bias=rbias[:, layer:layer + 1])\
                   .then_inc(S("logits_copied"), 1)
                token_rows(False)
                for k in range(2):
                    act.wait_ge(S("r_shifted"), 2 * layer + k + 1)
                    act.activation(M.a4[k], M.a4[k], ACT.Exp).then_inc(S("r_exp"), 1)
                act.wait_ge(S(f"route_done_l{layer}"), 1)
                n_pair = act.value_load(npair[0:1, 0:1], min_val=PAIRS, max_val=PAIRS + (MAX_EXTRA + 1) // 2)

                def gather_copies(done):
                    for q in range(4):
                        act.wait_ge(sm("gathered"), done * 4 + (q + 1))
                        copy(M.xsT[:, 512 * q:512 * (q + 1)], B[6 + q % 2][:, :]).then_inc(sm("gather_copied"), 1)

                def exp_gate(it, s):
                    slot, _, v = moe_unit(layer, 4 * s + 1, it)
                    act.wait_ge(free(layer, slot), v)
                    r = slice(64 * s, 64 * s + 64)
                    act.activation(M.ex[r, :], B[0][r, :], ACT.Exp, scale=-1.0).then_inc(sm("gate_exp"), 1)

                def hidden_copy(it, s):
                    act.wait_ge(sm("hidden_turned"), it * 2 + (s + 1))
                    copy(M.hT[:, 256 * s:256 * s + 256], B[3][:, 256 * s:256 * s + 256]).then_inc(sm("hidden_copied"), 1)

                def rows_out(it, s):
                    r = slice(64 * s, 64 * s + 64)
                    for q in range(4):
                        if q < 3:
                            act.wait_ge(sm("down_ready"), it * 6 + (3 * s + q + 1))
                        else:
                            slot, _, v = moe_unit(layer, 9 + 2 * s, it)
                            act.wait_ge(free(layer, slot), v)
                        copy(M.ys[r, 512 * q:512 * (q + 1)], B[4 + q % 2][r, :]).then_inc(sm("rows_out"), 1)

                act.wait_ge(sm("rows_out"), 1)
                act.wait_ge(sm("gt_copied"), 1)
                gather_copies(0)
                with act.Fori(0, n_pair) as it:
                    exp_gate(it, 0)
                    act.wait_ge(sm("gt_ready"), it + 1)
                    copy(M.gt, B[2][:, 0:T]).then_inc(sm("gt_copied"), 1)
                    exp_gate(it, 1)
                    hidden_copy(it, 0)
                    gather_copies(it + 1)
                    hidden_copy(it, 1)
                    rows_out(it, 0)
                    rows_out(it, 1)

            left(act, 0, "ln")
            copy(lnp[:, :], B[5][:, 0:P]).then_inc(S("lnp_copied"), 1)
            turn_rows(Xc, T)
            for layer in range(2):
                a = lay[layer]
                if layer == 0:
                    indexer(a)
                else:
                    forget_gates(a)
                for k in range(3):
                    slab(layer, "q", k, heads(a.qT[:, k * 4 * T:(k + 1) * 4 * T], 4), T, SCALE)
                if layer == 0:
                    slab(layer, "kv", 0, heads(a.kT, 2) + heads(a.vT, 2), T)
                else:
                    slab(layer, "kv", 0, heads(a.kT, 4), T)
                    slab(layer, "kv", 1, heads(a.vT, 4), T)
                slab(layer, "qm", 0, heads(a.qmT, 4), T, SCALE)
                pre = "a" if layer == 0 else "b"
                KN = a.KN[:, 0:2 * a.W].rearrange("p (t w) -> p t w", t=2)
                VN = a.VN.rearrange("p (t w) -> p t w", t=2)
                natural([(P, KN[:, 0, :]), (P, KN[:, 1, :]), (NB, a.KNs[:, 0:a.W])], a.W)
                act.wait_ge(S("natural_copied"), cnt["natural"])
                store(o[pre + "_k_p"][0, 0].rearrange("(t p) k d -> p t (k d)", p=P), KN)
                store(o[pre + "_k_s"][0].rearrange("b a k d -> (b a) (k d)"), a.KNs[:, 0:a.W])
                natural([(P, VN[:, 0, :]), (P, VN[:, 1, :]), (NB, a.VNs)], a.W)
                act.wait_ge(S("natural_copied"), cnt["natural"])
                store(o[pre + "_v_p"][0, 0].rearrange("(t p) k d -> p t (k d)", p=P), VN)
                store(o[pre + "_v_s"][0].rearrange("b a k d -> (b a) (k d)"), a.VNs)
                if layer == 1:
                    for j in range(4):
                        act.wait_ge(S("lf_turned"), j + 1)
                        copy(a.S[0:96, 512 * j:512 * j + 512], B[j][0:96, :]).then_inc(S("lf_copied"), 1)
                turn_rows(Ac, SEQ)
                slab(layer, "mkv", 0, heads(a.memK, 4, SEQ), SEQ)
                slab(layer, "mkv", 1, heads(a.mvT, 4, SEQ), SEQ)
                act.wait_ge(S("stored"), 16 * stores[0])
                if layer == 0:
                    act.wait_ge(S("ixp_added"), 16)
                MN = a.KN.rearrange("p (t w) -> p t w", t=2)
                MV = a.memV.rearrange("p (t w) -> p t w", t=2)
                natural([(P, MN[:, 0, :]), (P, MN[:, 1, :])], 512)
                natural([(P, MV[:, 0, :]), (P, MV[:, 1, :])], 512)
                act.wait_ge(S("natural_copied"), cnt["natural"])
                store(o["mem_k_p"][layer, 0].rearrange("(t p) k d -> p t (k d)", p=P), MN)
                store(o["mem_v_p"][layer, 0].rearrange("(t p) k d -> p t (k d)", p=P), MV)
                act.sem_inc(S("memory_done"), 1)
                pad_queries(layer, a)
                act.wait_ge(S("stored"), 16 * stores[0])
                sample_scores(layer, a)
                prompt_attention(layer, a)
                sample_attention(layer, a)
                left(act, layer, "r")
                copy(wr[:, :].rearrange("p (c a j) -> p c a j", a=5, j=4),
                     B[6][:, 0:320].rearrange("p (j a c) -> p c a j", a=5, c=KC)).then_inc(S("wr_copied"), 1)
                layer_norm(2 * layer)
                experts(layer)
                layer_norm(2 * layer + 1)
            token_rows(True)

        @block.vector
        def _(dve):
            chain = [0]

            def link(ins):
                chain[0] += 1
                ins.then_inc(S("dve_chain"), 1)
                dve.wait_ge(S("dve_chain"), chain[0])

            def top_k(sc, m8, k):
                for _ in range(k // 8):
                    link(dve.max(m8, sc))
                    link(dve.match_replace(sc, m8, sc, TAKEN))

            def prompt_index(a):
                for n in range(16):
                    t, c = divmod(n, 8)
                    dve.wait_ge(S("ixp_relu"), n + 1)
                    if n == 0:
                        dve.wait_ge(S("kiwi_rows_copied"), 3)
                    acc = a.MASK[:, t * SEQ:(t + 1) * SEQ]
                    for s in range(2):
                        w = a.nat[:, 192 + IH * t + 2 * c + s:193 + IH * t + 2 * c + s]
                        rl = a.RL[:, 512 * (n % 2) + SEQ * s:512 * (n % 2) + SEQ * (s + 1)]
                        if c == 0 and s == 0:
                            link(dve.tensor_scalar(acc, rl, w, None, ALU.mult))
                        elif s == 0:
                            link(dve.scalar_tensor_tensor(acc, rl, w, acc, ALU.mult, ALU.add))
                        else:
                            dve.scalar_tensor_tensor(acc, rl, w, acc, ALU.mult, ALU.add)\
                               .then_inc(S("ixp_added"), 1)
                            dve.wait_ge(S("ixp_added"), n + 1)

            def sample_topk(a):
                dve.wait_ge(S("ix_rows_copied"), 5)
                sc = a.S[96:96 + NB, 0:L1]
                top_k(sc, a.m8[96:96 + NB, :], TOPK_S)
                dve.tensor_scalar(sc, sc, -2e38, NEG, ALU.is_gt, ALU.mult).then_inc(S("mask_ready"), 1)

            def prompt_topk(a):
                for t in range(2):
                    m = a.MASK[:, t * SEQ:(t + 1) * SEQ]
                    causal = cst("causal")[:, t * SEQ:(t + 1) * SEQ]
                    link(dve.tensor_tensor(m, m, causal, ALU.add))
                    top_k(m, a.m8, TOPK_P)
                    link(dve.tensor_scalar(m, m, -2e38, NEG, ALU.is_gt, ALU.mult))
                    link(dve.tensor_tensor(m, m, causal, ALU.add))

            def forget_gates(a):
                dve.wait_ge(S("f_biased"), 1)
                dve.scalar_tensor_tensor(a.fe, a.fx, -1.0, a.fx, ALU.mult, ALU.max).then_inc(S("f_abs"), 1)
                dve.wait_ge(S("f_abs"), 1)
                dve.wait_ge(S("f_ln"), 1)
                link(dve.tensor_scalar(a.fx, a.fx, 0.0, None, ALU.min))
                link(dve.tensor_tensor(a.fx, a.fx, a.fe, ALU.subtract))
                dve.sem_inc(S("lf_ready"), 1)
                zero = cst("causal", H)[:, 0:1].broadcast_to((H, SEQ))
                link(dve.tensor_tensor_scan(a.fe[:, 0:SEQ], a.fx[:, 0:SEQ], zero, 0.0, ALU.add, ALU.add))
                link(dve.tensor_scalar(a.fe[:, 0:SEQ], a.fe[:, 0:SEQ], -1.0, None, ALU.mult))
                dve.sem_inc(S("lf_ready"), 1)
                dve.wait_ge(S("lf_rows"), 1)
                link(dve.tensor_tensor(a.own, B[6][0:96, 0:8], cst("own12", 96), ALU.mult))
                link(dve.tensor_reduce(a.st[0:96, 12:13], a.own, AX.X, ALU.add))
                dve.sem_inc(S("lf_rows_copied"), 1)

            def cached_gates(a):
                dve.wait_ge(S("lf_copied"), 4)
                link(dve.tensor_copy(a.S[0:96, PAST:L1], a.st[0:96, 12:13]))
                zero = cst("causal", 96)[:, 0:1].broadcast_to((96, L1))
                link(dve.tensor_tensor_scan(a.S[0:96, 0:L1], a.S[0:96, 0:L1], zero, 0.0, ALU.add, ALU.add))
                link(dve.tensor_copy(a.st[0:96, 13:14], a.S[0:96, PAST:L1]))
                link(dve.tensor_scalar(a.S[0:96, 0:L1], a.S[0:96, 0:L1], -1.0, a.st[0:96, 13:14], ALU.mult, ALU.add))

            def add_scores(layer, a):
                if layer == 0:
                    arrived(dve, 0, "ln")
                dve.wait_ge(S("k_scores"), layer + 1)
                for j in range(4):
                    r = a.S[0:96, 512 * j:512 * j + 512]
                    link(dve.tensor_tensor(r, B[j][0:96, :], r, ALU.add))
                link(dve.tensor_tensor(a.S[0:96, PAST:L1], B[6][0:96, 0:1], a.S[0:96, PAST:L1], ALU.add))
                dve.wait_ge(S("km_scores"), layer + 1)
                link(dve.tensor_copy(a.Sm, B[7][0:32, 0:SEQ]))
                dve.sem_inc(S("scores_added"), 1)

            def prompt_attention(layer, a):
                base = 16 * layer
                items = [("self", t, hp) for t in range(2) for hp in range(6)] + \
                        [("mem", t, hp) for t in range(2) for hp in range(2)]
                nm, rs = a.st[:, 0:4], a.st[:, 4:8]
                slope = slopes()
                for n in range(len(items) + 1):
                    if n < len(items):
                        kind, t, hp = items[n]
                        sc, ps = a.sc[n % 2], B[n % 2]
                        if kind == "self" and layer == 0:
                            for s in range(2):
                                link(dve.scalar_tensor_tensor(a.tb[:, s * SEQ:(s + 1) * SEQ],
                                                              cst("dist")[:, t * SEQ:(t + 1) * SEQ],
                                                              -float(np.float32(slope[2 * hp + s])),
                                                              a.MASK[:, t * SEQ:(t + 1) * SEQ], ALU.mult, ALU.add))
                        dve.wait_ge(S("p_scores"), base + n + 1)
                        if n >= 2:
                            dve.wait_ge(S("p_turned"), base + n - 1)
                        if kind == "mem":
                            link(dve.tensor_copy(sc, ps[:, :]))
                        elif layer == 0:
                            link(dve.tensor_tensor(sc, ps[:, :], a.tb, ALU.add))
                        else:
                            for s in range(2):
                                k = t * H + 2 * hp + s
                                link(dve.scalar_tensor_tensor(sc[:, s * SEQ:(s + 1) * SEQ],
                                                              ps[:, s * SEQ:(s + 1) * SEQ], a.cq[:, k:k + 1],
                                                              cst("causal")[:, t * SEQ:(t + 1) * SEQ],
                                                              ALU.add, ALU.add))
                        k = 2 * (n % 2)
                        dve.tensor_reduce(nm[:, k:k + 2], sc.rearrange("p (s k) -> p s k", s=2), AX.X, ALU.max,
                                          negate=True).then_inc(S("p_max"), 1)
                    if n >= 1:
                        m = n - 1
                        k = 2 * (m % 2)
                        dve.wait_ge(S("p_exp"), base + m + 1)
                        link(dve.reciprocal(rs[:, k:k + 2], rs[:, k:k + 2]))
                        for s in range(2):
                            x = a.sc[m % 2][:, s * SEQ:(s + 1) * SEQ]
                            e = dve.tensor_scalar(x, x, rs[:, k + s:k + s + 1], None, ALU.mult)
                        e.then_inc(S("p_norm"), 1)

            def sample_attention(layer, a):
                nm, rs = a.st[:, 8:10], a.st[:, 10:12]
                S_ = a.S[0:96, 0:L1]
                if layer == 0:
                    dve.wait_ge(S("mask_rows"), 1)
                    for j in range(4):
                        r = a.S[0:96, 512 * j:512 * j + 512]
                        link(dve.tensor_tensor(r, B[j][0:96, :], r, ALU.add))
                    link(dve.tensor_tensor(a.S[0:96, PAST:L1], B[4][0:96, 0:1], a.S[0:96, PAST:L1], ALU.add))
                link(dve.tensor_reduce(nm[0:96, 0:1], S_, AX.X, ALU.max, negate=True))
                dve.tensor_reduce(nm[0:32, 1:2], a.Sm, AX.X, ALU.max, negate=True).then_inc(S("s_max"), 1)
                dve.wait_ge(S("s_exp"), layer + 1)
                link(dve.reciprocal(rs[0:96, 0:1], rs[0:96, 0:1]))
                link(dve.reciprocal(rs[0:32, 1:2], rs[0:32, 1:2]))
                link(dve.tensor_scalar(S_, S_, rs[0:96, 0:1], None, ALU.mult))
                link(dve.tensor_scalar(a.Sm, a.Sm, rs[0:32, 1:2], None, ALU.mult))
                dve.tensor_scalar(a.epn, cst("own12", 96), a.S[0:96, PAST:L1], None, ALU.mult)\
                   .then_inc(S("s_norm"), 1)

            def mix(layer):
                for k in range(4):
                    left(dve, layer, "o", 2 * k + 1)
                    for f in range(4):
                        c = 4 * k + f
                        dve.scalar_tensor_tensor(Xc[c], Xc[c], ALPHA, B[4 * (k % 2) + f][:, 0:T], ALU.mult, ALU.add)\
                           .then_inc(S("mixed"), 1)

            def layer_norm(k):
                dve.wait_ge(S("ln_mean"), k + 1)
                dve.wait_ge(S("mixed"), 16 * (k + 1))
                for c in range(KC):
                    dve.tensor_tensor(Xc[c], Xc[c], B[0][:, 0:T], ALU.subtract).then_inc(S("ln_centred"), 1)
                dve.wait_ge(S("ln_square_used"), 16 * (k + 1))
                dve.tensor_scalar(M.rstd, B[1][:, 0:T], EPS, None, ALU.add).then_inc(S("ln_var"), 1)
                dve.wait_ge(S("ln_std"), k + 1)
                link(dve.reciprocal(M.rstd, M.rstd))
                for c in range(KC):
                    dve.tensor_tensor(Xc[c], Xc[c], M.rstd, ALU.mult).then_inc(S("ln_normed"), 1)

            def route(layer):
                v3 = lambda x, n: x.rearrange("p (t k) -> p t k", k=n)
                b3 = lambda x, n: x.unsqueeze(2).broadcast_to((P, 3, n))
                dve.wait_ge(S("logit_rows"), layer + 1)
                dve.wait_ge(S("zeroed"), ZERO[2] if layer == 0 else ZERO[4])
                link(dve.tensor_copy(M.lg[:, 0:40], B[6][:, 0:40]))
                link(dve.tensor_copy(M.lg[0:NB, 40:60], B[6][0:NB, 40:60]))
                lg = v3(M.lg, 20)
                gp, ep, og, t4, o1, o2, tmp, el = [v3(x, 4) for x in M.a4]
                mx, sm_, pg, v2, w1, w2, den, f1 = M.c1[0:8]
                first = v3(cst("first"), 4)

                def one_hot(out, x, m):
                    link(dve.tensor_tensor(t4, x, b3(m, 4), ALU.is_equal))
                    link(dve.tensor_tensor(t4, t4, first, ALU.mult))
                    link(dve.tensor_reduce(f1, t4, AX.X, ALU.max))
                    link(dve.tensor_tensor(out, t4, b3(f1, 4), ALU.is_equal))

                link(dve.tensor_reduce(mx, lg[:, :, 0:4], AX.X, ALU.max))
                dve.tensor_tensor(gp, lg[:, :, 0:4], b3(mx, 4), ALU.subtract).then_inc(S("r_shifted"), 1)
                dve.wait_ge(S("r_exp"), 2 * layer + 1)
                link(dve.tensor_reduce(sm_, gp, AX.X, ALU.add))
                link(dve.tensor_reduce(mx, gp, AX.X, ALU.max))
                link(dve.reciprocal(pg, sm_))
                link(dve.tensor_tensor(pg, pg, mx, ALU.mult))
                one_hot(og, gp, mx)
                for g in range(4):
                    e = lg[:, :, 4 + 4 * g:8 + 4 * g]
                    w = og[:, :, g:g + 1].broadcast_to((P, 3, 4))
                    link(dve.tensor_tensor(el if g == 0 else tmp, e, w, ALU.mult))
                    if g:
                        link(dve.tensor_tensor(el, el, tmp, ALU.add))
                link(dve.tensor_reduce(mx, el, AX.X, ALU.max))
                dve.tensor_tensor(ep, el, b3(mx, 4), ALU.subtract).then_inc(S("r_shifted"), 1)
                dve.wait_ge(S("r_exp"), 2 * layer + 2)
                link(dve.tensor_reduce(mx, ep, AX.X, ALU.max))
                one_hot(o1, ep, mx)
                link(dve.scalar_tensor_tensor(ep, o1, -2.0, ep, ALU.mult, ALU.add))
                link(dve.tensor_reduce(v2, ep, AX.X, ALU.max))
                one_hot(o2, ep, v2)
                link(dve.tensor_tensor(den, mx, v2, ALU.add))
                link(dve.reciprocal(den, den))
                link(dve.tensor_tensor(den, den, pg, ALU.mult))
                link(dve.tensor_tensor(w1, mx, den, ALU.mult))
                link(dve.tensor_tensor(w2, v2, den, ALU.mult))
                link(dve.tensor_tensor(tmp, o1, b3(w1, 4), ALU.mult))
                link(dve.tensor_tensor(t4, o2, b3(w2, 4), ALU.mult))
                link(dve.tensor_tensor(tmp, tmp, t4, ALU.add))
                link(dve.tensor_tensor(o1, o1, o2, ALU.add))
                link(dve.tensor_tensor(o1, o1, b3(cst("valid"), 4), ALU.mult))
                sel, gate, slot = M.w16[0], M.w16[1], M.w16[2]
                for g in range(4):
                    w = og[:, :, g:g + 1].broadcast_to((P, 3, 4))
                    link(dve.tensor_tensor(v3(sel, 16)[:, :, 4 * g:4 * g + 4], o1, w, ALU.mult))
                    link(dve.tensor_tensor(v3(gate, 16)[:, :, 4 * g:4 * g + 4], tmp, w, ALU.mult))
                dve.sem_inc(S("chosen"), 1)
                dve.wait_ge(S("ranks"), layer + 1)
                link(dve.scalar_tensor_tensor(slot, B[7][:, 0:48], 1.0, sel, ALU.add, ALU.mult))
                link(dve.tensor_scalar(slot, slot, -1.0, None, ALU.add))
                link(dve.tensor_copy(M.cnt, B[7][:, 48:64]))
                n_ec, nx = NE * CHUNKS, ENTRIES - NE
                fl, pos, ord_, tmp64 = [x[:, 0:n_ec] for x in M.fl]
                cb = M.cnt.unsqueeze(2).broadcast_to((P, NE, CHUNKS))
                e2 = lambda x: x.rearrange("p (e c) -> p e c", c=CHUNKS)
                link(dve.tensor_tensor(e2(fl), cb, e2(cst("chunk_base")), ALU.is_gt))
                zero = cst("causal")[:, 0:1].broadcast_to((P, n_ec))
                link(dve.tensor_tensor_scan(pos, fl, zero, 0.0, ALU.add, ALU.add))
                link(dve.tensor_tensor(ord_, pos, fl, ALU.mult))
                link(dve.tensor_scalar(ord_, ord_, -1.0, None, ALU.add))
                ind = M.ind.rearrange("p (k j) -> p k j", j=n_ec)
                link(dve.tensor_tensor(ind, ord_.unsqueeze(1).broadcast_to((P, nx, n_ec)),
                                       cst("entry").unsqueeze(2).broadcast_to((P, nx, n_ec)), ALU.is_equal))
                link(dve.tensor_scalar(tmp64, cst("chunk_base"), -BIG, None, ALU.add))
                link(dve.memset(M.LB[:, 0:NE], 0.0))
                link(dve.tensor_copy(M.LE, cst("entry_expert")))
                ind2 = ind
                link(dve.tensor_tensor(ind2, ind, tmp64.unsqueeze(1).broadcast_to((P, nx, n_ec)), ALU.mult))
                link(dve.tensor_reduce(M.LB[:, NE:ENTRIES], ind2, AX.X, ALU.add))
                link(dve.tensor_scalar(M.LB[:, NE:ENTRIES], M.LB[:, NE:ENTRIES], BIG, None, ALU.add))
                link(dve.tensor_tensor(ind, ord_.unsqueeze(1).broadcast_to((P, nx, n_ec)),
                                       cst("entry").unsqueeze(2).broadcast_to((P, nx, n_ec)), ALU.is_equal))
                link(dve.tensor_tensor(ind, ind, cst("chunk_expert").unsqueeze(1).broadcast_to((P, nx, n_ec)), ALU.mult))
                link(dve.tensor_reduce(M.LE[:, NE:ENTRIES], ind, AX.X, ALU.add))
                link(dve.tensor_copy(ent[:, :], M.LE[0:1, :]))
                half = (MAX_EXTRA + 1) // 2
                for k in range(half):
                    link(dve.tensor_scalar(M.no[0:1, k:k + 1], pos[0:1, n_ec - 1:n_ec], 2.0 * k, None, ALU.is_gt))
                link(dve.tensor_reduce(M.no[0:1, 7:8], M.no[0:1, 0:half], AX.X, ALU.add))
                link(dve.tensor_scalar(npair[:, :], M.no[0:1, 7:8], float(PAIRS), None, ALU.add))
                dve.sem_inc(S(f"route_done_l{layer}"), 1)

            def experts(layer):
                sm = lambda name: S(f"{name}_l{layer}")
                route(layer)
                n_pair = dve.value_load(npair[0:1, 0:1], min_val=PAIRS, max_val=PAIRS + (MAX_EXTRA + 1) // 2)
                gate, slot = M.w16[1], M.w16[2]
                regs = [dve.alloc_register(f"expert{k}_l{layer}") for k in range(2)]
                v3 = lambda x, n: x.rearrange("p (t k) -> p t k", k=n)

                class Links:
                    per, base, n = LINKS_PER_PASS, 0, 0

                lk = Links()

                def link(ins, done):
                    lk.n += 1
                    ins.then_inc(sm("pass_chain"), 1)
                    dve.wait_ge(sm("pass_chain"), done * lk.per + (lk.base + lk.n))

                def choose(done, k):
                    dve.reg_load(regs, ent[0:1, bass.ds(k * 2, 2)] if not isinstance(k, int) else ent[0:1, 2 * k:2 * k + 2])
                    ee = [dve.snap(g, min_val=0, max_val=NE - 1) for g in regs]
                    for s in range(2):
                        lb = M.LB[:, bass.ds(k * 2 + s, 1)]
                        link(dve.tensor_scalar(M.d3[:, 3 * s:3 * s + 3].unsqueeze(2), v3(slot, 16)[:, :, bass.ds(ee[s], 1)],
                                               lb, None, ALU.subtract), done)
                        out = M.sel.rearrange("p (t k) -> p t k", k=P)[:, :, 64 * s:64 * s + 64]
                        link(dve.tensor_tensor(out, cst("slot").unsqueeze(1).broadcast_to((P, 3, CAP)),
                                               M.d3[:, 3 * s:3 * s + 3].unsqueeze(2).broadcast_to((P, 3, CAP)),
                                               ALU.is_equal), done)
                        sg = M.sg.rearrange("p (t k) -> p t k", k=P)[:, :, 64 * s:64 * s + 64]
                        link(dve.tensor_tensor(sg, out,
                                               v3(gate, 16)[:, :, bass.ds(ee[s], 1)].broadcast_to((P, 3, CAP)),
                                               ALU.mult), done)
                    dve.tensor_copy(M.no[:, 0:1], M.no[:, 1:2]).then_inc(sm("chosen_slots"), 1)

                def scatter_add(it, c):
                    dve.wait_ge(sm("scattered"), it * 16 + (c + 1))
                    b = B[2] if c % 2 == 0 else B[6]
                    dve.tensor_tensor(Ac[c], b[:, 0:T], Ac[c], ALU.add).then_inc(sm("scatter_added"), 1)

                def hidden(it, s):
                    r = slice(64 * s, 64 * s + 64)
                    dve.wait_ge(sm("gate_exp"), it * 2 + (s + 1))
                    link(dve.tensor_scalar(M.ex[r, :], M.ex[r, :], 1.0, None, ALU.add), it)
                    link(dve.reciprocal(M.ex[r, :], M.ex[r, :]), it)
                    link(dve.tensor_tensor(M.ex[r, :], B[0][r, :], M.ex[r, :], ALU.mult), it)
                    slot_, _, v = moe_unit(layer, 4 * s + 3, it)
                    dve.wait_ge(free(layer, slot_), v)
                    dve.tensor_tensor(M.hh[r, :], B[1][r, :], M.ex[r, :], ALU.mult).then_inc(sm("hidden"), 1)

                link(dve.memset(M.no, 0.0), 0)
                choose(0, 0)
                lk.base, lk.n = lk.n, 0
                with dve.Fori(0, n_pair) as it:
                    for c in range(KC):
                        scatter_add(it, c)
                    hidden(it, 0)
                    dve.wait_ge(sm("gt_ready"), it + 1)
                    choose(it, it + 1)
                    hidden(it, 1)
                assert lk.n == LINKS_PER_PASS, lk.n
                for c in range(KC):
                    scatter_add(n_pair, c)
                dve.wait_ge(sm("scatter_added"), n_pair * 16 + 16)
                for c in range(KC):
                    dve.scalar_tensor_tensor(Xc[c], Xc[c], ALPHA, Ac[c], ALU.mult, ALU.add).then_inc(S("mixed"), 1)

            dve.wait_ge(S("consts_in"), 16)
            for layer in range(2):
                a = lay[layer]
                if layer == 0:
                    dve.wait_ge(S("wblock"), 1)
                    dve.tensor_tensor(a.Wb, B[7][:, 0:NB], cst("own16"), ALU.mult).then_inc(S("wblock_copied"), 1)
                    prompt_index(a)
                    sample_topk(a)
                    prompt_topk(a)
                else:
                    forget_gates(a)
                    cached_gates(a)
                add_scores(layer, a)
                prompt_attention(layer, a)
                sample_attention(layer, a)
                mix(layer)
                layer_norm(2 * layer)
                experts(layer)
                layer_norm(2 * layer + 1)
        assert stores[0] == N_STORES, stores[0]


QI_AT = H * P + 2 * 256
N_STORES = 2 + 4 + 2 + 2 + 4 + 2 + 3
LINKS_PER_PASS = 12

_INS = ['x_prompt', 'x_sample', 'mem_prompt', 'cache_a_k', 'cache_a_v', 'cache_a_ik', 'cache_b_k', 'cache_b_v',
        'cache_b_lf', 'cache_mem_k', 'cache_mem_v', 'page_table', 'w_in_a', 'w_in_b', 'b_f', 'w_mem_kv', 'w_o',
        'ln1_g', 'ln1_b', 'ln2_g', 'ln2_b', 'w_r1', 'b_r1', 'w_r2', 'b_r2', 'w_gate', 'w_up', 'w_down']
_OUTS = [("y_prompt", (1, SEQ, D)), ("y_sample", (NB, 1, D)),
         ("a_k_p", (1, 1, SEQ, 2, P)), ("a_v_p", (1, 1, SEQ, 2, P)), ("a_ik_p", (1, 1, SEQ, 64)),
         ("b_k_p", (1, 1, SEQ, 4, P)), ("b_v_p", (1, 1, SEQ, 4, P)), ("b_lf_p", (1, 1, SEQ, H)),
         ("mem_k_p", (2, 1, 256, HM, P)), ("mem_v_p", (2, 1, 256, HM, P)),
         ("a_k_s", (1, NB, 1, 2, P)), ("a_v_s", (1, NB, 1, 2, P)), ("a_ik_s", (1, NB, 1, 64)),
         ("b_k_s", (1, NB, 1, 4, P)), ("b_v_s", (1, NB, 1, 4, P)), ("b_lf_s", (1, NB, 1, H))]


def kernel(**inputs):
    import concourse.bacc as bacc
    from concourse.bass_utils import run_bass_kernel_spmd

    nc = bacc.Bacc("TRN2", target_bir_lowering=False, num_devices=1)
    arrays, i, o = {}, {}, {}
    given = {name: inputs[name] for name in _INS}
    given["consts"] = CONSTS
    given["alibi"] = alibi_rows()
    for name, a in given.items():
        a = np.ascontiguousarray(a)
        arrays[f"in_{name}"] = a
        i[name] = nc.dram_tensor(f"in_{name}", a.shape, mybir.dt.from_np(a.dtype), kind="ExternalInput").ap()
    for name, shape in _OUTS:
        o[name] = nc.dram_tensor(f"out_{name}", shape, F32, kind="ExternalOutput").ap()
    step_kernel(nc, i, o)
    r = run_bass_kernel_spmd(nc, [arrays], core_ids=[0])
    return tuple(r.results[0][f"out_{name}"] for name, _ in _OUTS)
```

```python
import concourse.bass as bass
from concourse import mybir
from contextlib import ExitStack
import numpy as np

F32 = mybir.dt.float32
BF16 = mybir.dt.bfloat16
I32 = mybir.dt.int32
ALU = mybir.AluOpType
ACT = mybir.ActivationFunctionType
AX = mybir.AxisListType

P = 128
D = 2048
KC = D // P
SEQ = 256
NB = 8
T = SEQ + NB
PAGES = 16
PAST = PAGES * P
L1 = PAST + 1
N_POOL = 160
H = 12
HM = 4
IH = 16
TOPK_P, TOPK_S = 64, 256
SCALE = float(np.float32(P ** -0.5))
NEG = -1e30
TAKEN = -3e38
ALPHA = 4 ** 0.25
EPS = 1e-5
NE = 16
FE = 512
CAP = 64
PAIRS = NE // 2
MAX_EXTRA = 2 * T // (CAP + 1)
ENTRIES = 2 * (PAIRS + (MAX_EXTRA + 1) // 2 + 1)
CHUNKS = -(-T // CAP) - 1
RING, UNIT = 6, 4096
COLS_A, COLS_B = 3664, 3084
IK_EARLY = 6

CONST = {}


def const_table():
    parts, at = [], 0

    def add(name, a):
        nonlocal at
        full = np.zeros((P, a.shape[1]), np.float32)
        full[:a.shape[0]] = a
        CONST[name] = (at, a.shape[1])
        parts.append(full)
        at += a.shape[1]

    i = np.arange(P)
    add("ident", np.eye(P))
    add("mean", np.full((P, P), 1.0 / D))
    add("ones", np.ones((P, P)))
    add("before", (i[:, None] < i[None, :]).astype(np.float32))
    k = np.arange(SEQ)
    add("causal", np.concatenate([np.where(k[None] <= (i + P * t)[:, None], 0.0, NEG) for t in range(2)], 1))
    add("dist", np.concatenate([(i + P * t)[:, None] - k[None] for t in range(2)], 1))
    add("slot", np.broadcast_to(np.arange(CAP), (P, CAP)))
    rep16 = np.zeros((IH, P))
    rep16[np.arange(P) % IH, i] = 1
    add("rep16", rep16)
    add("own16", (i[:, None] // IH == np.arange(NB)[None]).astype(np.float32))
    r = np.arange(NB * H)
    rep12 = np.zeros((H, NB * H))
    rep12[r % H, r] = 1
    add("rep12", rep12)
    own12 = (r[:, None] // H == np.arange(NB)[None]).astype(np.float32)
    add("own12", own12)
    to12 = np.zeros((P, NB * H))
    to12[96:96 + NB] = own12.T
    add("to12", to12)
    add("fold12", (i[:, None] % 32 == np.arange(H)[None]).astype(np.float32))
    j = np.arange(2 * HM)
    add("fold4", ((i[:, None] % 32 == j[None] % HM) & (i[:, None] // 64 == j[None] // HM)).astype(np.float32))
    add("first", np.broadcast_to(np.tile([4.0, 3.0, 2.0, 1.0], 3), (P, 12)))
    add("valid", np.stack([np.ones(P), np.ones(P), i < NB], 1))
    e, c = np.divmod(np.arange(NE * CHUNKS), CHUNKS)
    add("chunk_base", np.broadcast_to(CAP * (c + 1.0), (P, NE * CHUNKS)))
    add("chunk_expert", np.broadcast_to(e.astype(np.float32), (P, NE * CHUNKS)))
    add("entry_expert", np.broadcast_to(np.where(np.arange(ENTRIES) < NE, np.arange(ENTRIES), 0), (P, ENTRIES)))
    add("entry", np.broadcast_to(np.arange(ENTRIES - NE), (P, ENTRIES - NE)))
    return np.concatenate(parts, 1).astype(np.float32)


def slopes():
    def pow2(m):
        return [(2.0 ** (-8.0 / m)) ** (j + 1) for j in range(m)]
    return pow2(8) + pow2(16)[0::2][:H - 8]


def alibi_rows():
    s = np.tile(np.asarray(slopes(), np.float32), NB)
    return -(s[:, None] * (PAST - np.arange(L1, dtype=np.float32))[None]).astype(np.float32)


CONSTS = const_table()
NC_CONST = CONSTS.shape[1]
BIG = 4096.0


class Ring:

    def __init__(self, start=0):
        self.n = start
        self.full = [0] * RING
        self.used = [0] * RING

    def take(self, n_dma=1):
        s = self.n % RING
        self.n += 1
        before = self.used[s]
        self.full[s] += 16 * n_dma
        self.used[s] += 1
        return s, self.full[s], self.used[s], before


def plan(layer):
    u = []
    if layer == 0:
        u += [("ln", 0, 5), ("x", 0, 1), ("xs", 0, 1), ("kiwi", 0, 2), ("qi", 0, 1), ("qi", 1, 1), ("qi", 2, 1),
              ("qi", 3, 1), ("ik", 0, 16 * (NB - IK_EARLY))]
    else:
        u += [("f", 0, 1)]
    u += [("q", k, 1) for k in range(6)]
    u += [("kv", k, 1) for k in range(2 if layer == 0 else 4)]
    u += [("qm", k, 1) for k in range(2)]
    u += [("mem", 0, 1)] + [("mkv", k, 1) for k in range(4)]
    n = 8 if layer == 0 else 16
    u += [("k", k, 128 // n) for k in range(n)] + [("mk", k, 4) for k in range(2)]
    u += [("v", k, 128 // n) for k in range(n)] + [("mv", k, 4) for k in range(2)]
    u += [("r", 0, 5)] + [("o", k, 1) for k in range(8)]
    return u


def step_kernel(nc, i, o):
    with ExitStack() as ctx:
        sems = {}

        def S(name):
            if name not in sems:
                sems[name] = ctx.enter_context(nc.semaphore(name))
            return sems[name]

        def sb(name, cols, dt=F32, rows=P):
            return ctx.enter_context(nc.sbuf_tensor(name, [rows, cols], dt))

        ring = [sb(f"ring{k}", UNIT) for k in range(RING)]
        X = sb("X", KC * T)
        AT = sb("AT", KC * T)
        consts = sb("consts", NC_CONST)
        lnp = sb("lnp", 128)
        rbias = sb("rbias", 2, rows=20)
        fbias = sb("fbias", 1, rows=H)
        ptab = sb("ptab", NB * PAGES, I32, rows=1)
        wr = sb("wr", KC * 20)
        ARENA = 17416
        arena = sb("arena", ARENA)
        B = [ctx.enter_context(nc.psum_tensor(f"bank{k}", [P, 512], F32)) for k in range(8)]

        def cst(name, rows=P, lo=0):
            a, n = CONST[name]
            return consts[lo:lo + rows, a:a + n]

        ident = cst("ident")

        def ar(at, n, rows=P):
            return arena[0:rows, at:at + n]

        Xc = [X[:, c * T:(c + 1) * T] for c in range(KC)]
        Ac = [AT[:, c * T:(c + 1) * T] for c in range(KC)]
        Xv = X[:, :].rearrange("p (c t) -> p c t", t=T)
        Av = AT[:, :].rearrange("p (c t) -> p c t", t=T)

        class Lay:
            pass

        lay = []
        for layer in range(2):
            a = Lay()
            nk = a.nk = 2 if layer == 0 else 4
            a.G = H // nk
            a.W = nk * P
            at = 0

            def place(n, rows=P):
                nonlocal at
                at += n
                assert at <= ARENA, at
                return ar(at - n, n, rows)

            a.qT = place(H * T)
            a.PT = ar(0, PAGES * 96)
            a.PTm = ar(PAGES * 96, 64)
            a.IK = ar(0, IK_EARLY * PAGES * 64)
            a.PTn = ar(PAGES * 96 + 64, 96, NB)
            a.epn = ar(PAGES * 96 + 160, NB, 96)
            a.qmT = place(HM * T)
            a.kT = place(nk * T)
            if layer == 0:
                a.vT = place(nk * T)
            a.VN = place(2 * a.W)
            a.VNs = place(a.W, NB)
            a.memK = place(HM * SEQ)
            a.memV = place(2 * 512)
            a.S = place(L1 + 3)
            if layer == 1:
                a.vT = a.S[:, 0:nk * T]
            a.KTs = place(1024)
            a.KN = a.KTs
            a.Qz = place(3072)
            a.qiT = a.Qz
            a.sc = [a.Qz[:, 512 * k:512 * k + 512] for k in (0, 1, 4)]
            a.PTp = [a.Qz[:, 1024 + 512 * k:1536 + 512 * k] for k in range(2)]
            a.LF = a.Qz[:, 0:PAGES * 96]
            a.Qmz = place(HM * NB * 32)
            a.QIz = a.Qmz
            a.mvT = a.Qmz
            a.Sm = place(SEQ, 32)
            if layer == 0:
                kiwi = place(2 * T)
                a.KI, a.WI = kiwi[:, 0:T], kiwi[0:IH, T:2 * T]
                a.KNs = kiwi[0:NB, 0:512]
                a.ovs = kiwi[:, 0:512]
                a.nat = place(224)
                a.MASK = place(512)
                a.tb = place(512)
                a.RL = a.memV
                a.Wb = place(NB)
                a.m8 = place(8)
            else:
                a.ovs = place(512)
                a.KNs = a.ovs[0:NB, :]
                a.fx = place(T, H)
                a.fe = place(T, H)
                a.cq = place(24)
                a.lfn = place(36)
                a.own = place(NB, 96)
            a.st = place(16)
            lay.append(a)

        M = Lay()
        at = 0
        parts = ar(at, 9 * D // 2).bitcast(BF16)
        M.part = [[parts[:, (3 * t + k) * D:(3 * t + k + 1) * D] for k in range(3)] for t in range(3)]
        M.xtok = ar(at, 3 * D); at += 9 * D // 2
        M.xsT = ar(at, KC * P); at += KC * P
        M.ys = ar(at, D)
        M.rest = [ar(at + 512 * k, 512) for k in range(4)]; at += D
        M.sel = ar(at, 3 * P // 2).bitcast(BF16); at += 3 * P // 2
        M.sg = ar(at, 3 * P); at += 3 * P
        M.gt = ar(at, T); at += T
        M.sq = [ar(at, T), ar(at + T, T)]
        M.rstd = ar(at + 2 * T, T)
        M.ind = ar(at + 3 * T, (ENTRIES - NE) * NE * CHUNKS)
        assert 3 * T + (ENTRIES - NE) * NE * CHUNKS <= 1536
        M.ex = ar(at, 512); at += 512
        M.hh = ar(at, 512); at += 512
        M.hT = ar(at, 512); at += 512
        M.lgT = ar(at, T, 20); at += T
        M.lg = ar(at, 60); at += 60
        M.a4 = [ar(at + 12 * k, 12) for k in range(8)]; at += 96
        M.w16 = [ar(at + 48 * k, 48) for k in range(4)]; at += 192
        M.c1 = [ar(at + 3 * k, 3) for k in range(12)]; at += 36
        M.cnt = ar(at, 16); at += 16
        M.fl = [ar(at + 64 * k, 64) for k in range(4)]; at += 256
        M.LB = ar(at, ENTRIES); at += ENTRIES
        M.LE = ar(at, ENTRIES); at += ENTRIES
        NX = ENTRIES - NE
        M.d3 = ar(at, 6); at += 6
        M.no = ar(at, 8); at += 8
        assert at <= ARENA, at
        ent = sb("entries", ENTRIES, I32, rows=1)
        npair = sb("npair", 1, I32, rows=1)

        units = []
        starts = []
        r = Ring()
        moe_at = []
        for layer in range(2):
            if layer:
                r = Ring(r.n + 12 * PAIRS)
            at_l = {}
            for name, k, n in plan(layer):
                at_l[name, k] = r.take(n)
            units.append(at_l)
            moe_at.append((r.n, list(r.full), list(r.used)))

        def full(layer, s):
            return S(f"full{s}_l{layer}")

        def free(layer, s):
            return S(f"free{s}_l{layer}")

        def arrived(eng, layer, name, k=0):
            s, v, _, _ = units[layer][name, k]
            eng.wait_ge(full(layer, s), v)
            return ring[s]

        def leave(mm, layer, name, k=0):
            mm.then_inc(free(layer, units[layer][name, k][0]), 1)

        def left(eng, layer, name, k=0):
            s, _, v, _ = units[layer][name, k]
            eng.wait_ge(free(layer, s), v)

        def moe_unit(layer, k, it):
            n0, f0, u0 = moe_at[layer]
            s = (n0 + k) % RING
            return s, it * 32 + (f0[s] + 16 * (k // RING + 1)), it * 2 + (u0[s] + k // RING + 1)

        def load_pages(eng, regs, sem, b, first, n, cache, dst):
            for g in range(first, first + n, 8):
                eng.reg_load(regs, ptab[0:1, b * PAGES + g:b * PAGES + g + 8])
                for k in range(8):
                    page = eng.snap(regs[k], min_val=0, max_val=N_POOL - 1)
                    eng.dma_start(dst(g + k), cache[bass.ds(page, 1)].rearrange("a p w -> (a p) w")).then_inc(sem, 16)

        def row_item(n):
            t, q = divmod(n - 1, 4)
            rows = P if t < 2 else NB
            return rows, t, [M.part[t][k][0:rows, 512 * q:512 * (q + 1)] for k in range(3)]

        block = ctx.enter_context(nc.Block())

        @block.sync
        def _(sp):
            sp.dma_start(consts[:, :], i["consts"]).then_inc(S("consts_in"), 16)
            sp.dma_start(ptab[:, :], i["page_table"].rearrange("(a b) c -> a (b c)", a=1)).then_inc(S("table_in"), 16)
            for layer in range(2):
                sp.dma_start(rbias[0:4, layer:layer + 1],
                             i["b_r1"][layer].rearrange("(a b) -> a b", b=1)).then_inc(S("bias_in"), 16)
                sp.dma_start(rbias[4:20, layer:layer + 1],
                             i["b_r2"][layer].rearrange("g (e b) -> (g e) b", b=1)).then_inc(S("bias_in"), 16)
            sp.dma_start(fbias[:, :], i["b_f"][0].rearrange("(a b) -> a b", b=1)).then_inc(S("bias_in"), 16)
            sp.wait_ge(S("table_in"), 16)
            pregs = [sp.alloc_register(f"page{k}") for k in range(8)]

            def pages(layer, s, b, first, n, cache, dst):
                load_pages(sp, pregs, full(layer, s), b, first, n, cache, dst)

            def wload(layer, s, w, half, c0, n, at=0, width=None):
                width = width or n
                rows = w.rearrange("(c p) f -> p c f", p=P)
                k = KC // 2 if half is not None else KC
                c = (half or 0) * k
                dst = ring[s][:, 0:k * width].rearrange("p (c f) -> p c f", f=width)[:, :, at:at + n]
                sp.dma_start(dst, rows[:, c:c + k, c0:c0 + n]).then_inc(full(layer, s), 16)

            for layer in range(2):
                win = i["w_in_a"][0] if layer == 0 else i["w_in_b"][0]
                ck = i["cache_a_k" if layer == 0 else "cache_b_k"][0].rearrange("n p k d -> n p (k d)")
                cv = i["cache_a_v" if layer == 0 else "cache_b_v"][0].rearrange("n p k d -> n p (k d)")
                W = 256 if layer == 0 else 512
                col_kv, col_qm = H * P, (COLS_A if layer == 0 else COLS_B) - HM * P
                if layer == 1:
                    sp.wait_ge(S("route_done_l0"), 1)
                    n_pair = sp.value_load(npair[0:1, 0:1], min_val=PAIRS, max_val=PAIRS + (MAX_EXTRA + 1) // 2)
                    waited = set()
                for name, k, n_dma in plan(layer):
                    s, _, _, before = units[layer][name, k]
                    if before:
                        sp.wait_ge(free(layer, s), before)
                    elif layer == 1:
                        n0, _, u0 = moe_at[0]
                        sp.wait_ge(free(0, s), n_pair * 2 + u0[s])
                    t = ring[s]
                    if name == "ln":
                        for a, w in enumerate(("ln1_g", "ln1_b", "ln2_g", "ln2_b")):
                            sp.dma_start(t[32 * a:32 * a + 32, 0:P], i[w].rearrange("l (c p) -> (l c) p", p=P))\
                              .then_inc(full(layer, s), 16)
                        sp.dma_start(lay[0].S[0:96, 0:L1], i["alibi"]).then_inc(full(layer, s), 16)
                    elif name == "x" or name == "mem":
                        x = i["x_prompt" if name == "x" else "mem_prompt"][0]
                        sp.dma_start(t[:, :].rearrange("p (a d) -> p a d", a=2),
                                     x.rearrange("(a p) d -> p a d", p=P)).then_inc(full(layer, s), 16)
                    elif name == "xs":
                        sp.dma_start(t[0:NB, 0:D], i["x_sample"].rearrange("b a d -> (b a) d"))\
                          .then_inc(full(layer, s), 16)
                    elif name == "kiwi":
                        c0 = QI_AT + IH * 64
                        wload(layer, s, win, None, c0, 64, 0, 144)
                        wload(layer, s, win, None, c0, 80, 64, 144)
                    elif name == "f":
                        wload(layer, s, win, None, H * P + 2 * W, H)
                    elif name in ("qi", "q", "kv", "qm"):
                        c0 = {"qi": QI_AT, "q": 0, "kv": col_kv, "qm": col_qm}[name]
                        wload(layer, s, win, k % 2, c0 + 512 * (k // 2), 512)
                    elif name == "mkv":
                        wload(layer, s, i["w_mem_kv"][layer], k % 2, 512 * (k // 2), 512)
                    elif name == "o":
                        wload(layer, s, i["w_o"][layer], k % 2, 512 * (k // 2), 512)
                    elif name == "ik":
                        for b in range(IK_EARLY, NB):
                            pages(layer, s, b, 0, PAGES, i["cache_a_ik"][0],
                                  lambda g: t[:, ((b - IK_EARLY) * PAGES + g) * 64:((b - IK_EARLY) * PAGES + g + 1) * 64])
                    elif name in ("k", "v"):
                        per = UNIT // W
                        b, first = divmod(k * per, PAGES)
                        pages(layer, s, b, first, per, ck if name == "k" else cv,
                              lambda g: t[:, (g - first) * W:(g - first + 1) * W])
                    elif name in ("mk", "mv"):
                        c = i["cache_mem_k" if name == "mk" else "cache_mem_v"][layer]
                        for b in range(4):
                            sp.dma_start(t[:, b * 1024:(b + 1) * 1024].rearrange("p (a w) -> p a w", a=2),
                                         c[4 * k + b].rearrange("(a p) h d -> p a (h d)", p=P))\
                              .then_inc(full(layer, s), 16)
                    elif name == "r":
                        sp.dma_start(t[0:16, 0:512], i["w_r1"][layer].rearrange("(c p) j -> c (p j)", p=P))\
                          .then_inc(full(layer, s), 16)
                        for g in range(4):
                            sp.dma_start(t[16 + 16 * g:32 + 16 * g, 0:512],
                                         i["w_r2"][layer, g].rearrange("(c p) j -> c (p j)", p=P))\
                              .then_inc(full(layer, s), 16)
                wg, wu, wd = (i[n][layer] for n in ("w_gate", "w_up", "w_down"))

                def pass_loads(it, experts):
                    for k in range(12):
                        s, _, freed = moe_unit(layer, k, it)
                        sp.wait_ge(free(layer, s), freed - 1)
                        half, e = k // 2 % 2, experts[k % 2]
                        if k < 8:
                            w = (wg if k < 4 else wu)[bass.ds(e, 1)]
                            src = w.rearrange("a (c p) f -> p (a c) f", p=P)[:, 8 * half:8 * half + 8, :]
                            dst = ring[s][:, :].rearrange("p (c f) -> p c f", f=FE)
                        else:
                            w = wd[bass.ds(e, 1)]
                            src = w.rearrange("a (c p) f -> p (a c) f", p=P)[:, :, D // 2 * half:D // 2 * (half + 1)]
                            dst = ring[s][:, :].rearrange("p (c f) -> p c f", f=D // 2)
                        sp.dma_start(dst, src).then_inc(full(layer, s), 16)

                with sp.Fori(0, PAIRS) as it:
                    pass_loads(it, (it * 2, it * 2 + 1))
                sp.wait_ge(S(f"route_done_l{layer}"), 1)
                n_all = sp.value_load(npair[0:1, 0:1], min_val=PAIRS, max_val=PAIRS + (MAX_EXTRA + 1) // 2)
                with sp.If(n_all > PAIRS):
                    with sp.Fori(PAIRS, n_all) as it:
                        sp.reg_load(pregs[0:2], ent[0:1, bass.ds(it * 2, 2)])
                        experts = [sp.snap(g, min_val=0, max_val=NE - 1) for g in pregs[0:2]]
                        pass_loads(it, experts)
            sp.wait_ge(S("stored"), 16 * N_STORES)

        @block.gpsimd
        def _(pool):
            for layer in range(2):
                a = lay[layer]
                if layer == 0:
                    pool.memset(a.QIz, 0.0).then_inc(S("zeroed"), 1)
                pool.wait_ge(S("memory_done"), layer + 1)
                pool.memset(a.Qz[:, 0:a.nk * NB * 96], 0.0).then_inc(S("zeroed"), 1)
                pool.memset(a.Qmz, 0.0).then_inc(S("zeroed"), 1)
                pool.wait_ge(S("mixed"), 16 * (2 * layer + 1))
                pool.memset(AT[:, :], 0.0).then_inc(S("zeroed"), 1)
                pool.memset(M.lg, 0.0).then_inc(S("zeroed"), 1)
                for n in range(1, 14):
                    if n <= 12:
                        rows, _, out = row_item(n)
                        pool.wait_ge(S("high_made"), 12 * layer + n)
                        rest = M.rest[n % 4][0:rows, :]
                        pool.tensor_tensor(rest, rest, out[0], ALU.subtract).then_inc(S("rest_made"), 1)
                    if n > 1:
                        rows, _, out = row_item(n - 1)
                        pool.wait_ge(S("mid_made"), 12 * layer + n - 1)
                        pool.tensor_tensor(out[2], M.rest[(n - 1) % 4][0:rows, :], out[1], ALU.subtract)\
                            .then_inc(S("low_made"), 1)
                pool.wait_ge(S("low_made"), 12 * (layer + 1))
                pool.memset(M.ys, 0.0).then_inc(S(f"rows_out_l{layer}"), 1)
                pool.memset(M.gt, 0.0).then_inc(S(f"gt_copied_l{layer}"), 1)
        ZERO = [1, 3, 5, 7, 9]

        @block.tensor
        def _(pe):
            cnt = {}

            def bump(name, k=1):
                cnt[name] = cnt.get(name, 0) + k
                return cnt[name]

            pe.wait_ge(S("consts_in"), 16)

            def turn_rows(layer, name):
                t = arrived(pe, layer, name)
                if name == "x":
                    ts = arrived(pe, layer, "xs")
                for c in range(KC):
                    n = bump("rows_turned")
                    if n > 4:
                        pe.wait_ge(S("rows_copied"), n - 4)
                    b = B[n % 4]
                    for g in range(2):
                        mm = pe.transpose(b[:, g * P:(g + 1) * P], t[:, g * D + c * P:g * D + (c + 1) * P], ident)
                    if name == "x":
                        mm = pe.transpose(b[:, SEQ:T], ts[0:NB, c * P:(c + 1) * P], ident[0:NB, 0:NB])
                    mm.then_inc(S("rows_turned"), 1)
                pe.wait_ge(S("rows_copied"), n)
                mm = pe.transpose(B[4][:, 0:P], ident, ident)
                leave(mm, layer, name)
                if name == "x":
                    mm = pe.transpose(B[4][:, 0:P], ident, ident)
                    leave(mm, layer, "xs")

            def slab(layer, name, k, src, n_tok):
                g = bump("slab")
                if g > 2:
                    pe.wait_ge(S("slab_copied"), g - 2)
                for half in range(2):
                    u = arrived(pe, layer, name, 2 * k + half)
                    for f in range(4):
                        for c in range(8):
                            mm = pe.matmul(B[4 * (g % 2) + f][:, 0:n_tok],
                                           u[:, c * 512 + f * P:c * 512 + (f + 1) * P],
                                           src[8 * half + c][:, 0:n_tok],
                                           start=(half == 0 and c == 0), stop=(half == 1 and c == 7))
                    leave(mm, layer, name, 2 * k + half)

            def slabs_done():
                pe.wait_ge(S("slab_copied"), cnt["slab"])

            def natural(src, nh, n_items, col=T):
                for t in range(n_items):
                    n = bump("natural")
                    if n > 2:
                        pe.wait_ge(S("natural_copied"), n - 2)
                    rows = P if t < 2 else NB
                    for h in range(nh):
                        mm = pe.transpose(B[4 + n % 2][0:rows, h * P:(h + 1) * P],
                                          src[:, h * col + t * P:h * col + t * P + rows], ident)
                    mm.then_inc(S("natural_ready"), 1)

            def memory(layer, a):
                slabs_done()
                turn_rows(layer, "mem")
                for k in range(2):
                    slab(layer, "mkv", k, Ac, SEQ)
                slabs_done()
                natural(a.memK, HM, 2, SEQ)
                natural(a.mvT, HM, 2, SEQ)
                pe.wait_ge(S("natural_copied"), cnt["natural"])

            def indexer(a):
                u = arrived(pe, 0, "kiwi")
                for c in range(KC):
                    pe.matmul(B[4][:, 0:T], u[:, c * 144:c * 144 + P], Xc[c], start=(c == 0), stop=(c == KC - 1))
                for c in range(KC):
                    mm = pe.matmul(B[5][0:IH, 0:T], u[:, c * 144 + P:c * 144 + 144], Xc[c],
                                   start=(c == 0), stop=(c == KC - 1))
                leave(mm, 0, "kiwi")
                pe.wait_ge(S("kiwi_copied"), 2)
                for t in range(2):
                    pe.transpose(B[6][:, 64 * t:64 * t + 64], a.KI[0:64, t * P:(t + 1) * P], ident[0:64, 0:64])
                    pe.transpose(B[6][:, 192 + IH * t:192 + IH * (t + 1)], a.WI[:, t * P:(t + 1) * P],
                                 ident[0:IH, 0:IH])
                pe.transpose(B[6][0:NB, P:P + 64], a.KI[0:64, SEQ:T], ident[0:64, 0:64]).then_inc(S("kiwi_rows"), 1)
                pe.matmul(B[7][:, 0:NB], cst("rep16", IH), a.WI[:, SEQ:T], start=True, stop=True)\
                  .then_inc(S("wblock"), 1)
                pe.wait_ge(S("kiwi_rows_copied"), 3)
                pe.wait_ge(S("wblock_copied"), 1)
                for k in range(2):
                    slab(0, "qi", k, Xc, T)
                slabs_done()
                for n in range(16):
                    t, c = divmod(n, 8)
                    if n >= 2:
                        pe.wait_ge(S("ixp_relu"), n - 1)
                    for s in range(2):
                        mm = pe.matmul(B[4 + 2 * (n % 2) + s][:, 0:SEQ],
                                       a.qiT[64 * s:64 * s + 64, c * T + t * P:c * T + (t + 1) * P],
                                       a.KI[64 * s:64 * s + 64, 0:SEQ], start=True, stop=True)
                    mm.then_inc(S("ixp_scores"), 1)
                pe.wait_ge(S("qiz_built"), 2)
                pe.wait_ge(S("ixp_relu"), 16)
                pe.wait_ge(S("ik_in"), 16 * PAGES * IK_EARLY)
                late = arrived(pe, 0, "ik")

                def product(n):
                    j, b = divmod(n, NB)
                    pe.wait_ge(S("kt_copied"), n + 1)
                    if b == 0 and j >= 2:
                        pe.wait_ge(S("ix_relu"), j - 1)
                    mm = pe.matmul(B[2 + j % 2][:, :], a.QIz[:, b * P:(b + 1) * P],
                                   a.KTs[:, 512 * (n % 2):512 * (n % 2) + 512], start=(b == 0), stop=(b == NB - 1))
                    if b == NB - 1:
                        mm.then_inc(S("ix_scores"), 1)

                def rows(j):
                    w = 512 if j < 4 else 1
                    pe.wait_ge(S("ix_relu"), j + 1)
                    if j:
                        pe.wait_ge(S("ix_rows_copied"), j)
                    pe.matmul(B[5][96:96 + NB, 0:w], a.Wb, a.tb[:, 0:w], start=True, stop=True)\
                      .then_inc(S("ix_rows"), 1)

                for n in range(32):
                    j, b = divmod(n, NB)
                    bump("kt")
                    if n >= 2:
                        pe.wait_ge(S("kt_copied"), n - 1)
                    for pg in range(4):
                        keys, at = (a.IK, b * PAGES * 64) if b < IK_EARLY else (late, (b - IK_EARLY) * PAGES * 64)
                        at += (4 * j + pg) * 64
                        for s in range(2):
                            mm = pe.matmul(B[n % 2][64 * s:64 * s + 64, pg * P:(pg + 1) * P],
                                           keys[:, at:at + 64], ident, start=True, stop=True)
                    mm.then_inc(S("kt_ready"), 1)
                    if n:
                        product(n - 1)
                        if n % NB == 1 and n > NB:
                            rows(j - 1)
                product(31)
                for b in range(NB):
                    if b == 0:
                        pe.wait_ge(S("ixp_relu"), 16)
                    mm = pe.matmul(B[4][:, 0:1], a.QIz[:, b * P:(b + 1) * P], a.KI[:, SEQ + b:SEQ + b + 1],
                                   start=(b == 0), stop=(b == NB - 1))
                    if b == 0:
                        leave(mm, 0, "ik")
                mm.then_inc(S("ix_scores"), 1)
                rows(3)
                rows(4)
                pe.wait_ge(S("ix_rows_copied"), 5)

            def forget_gates(a):
                u = arrived(pe, 1, "f")
                for c in range(KC):
                    pe.wait_ge(S("ln_out"), KC + c + 1)
                    mm = pe.matmul(B[4][0:H, 0:T], u[:, c * H:(c + 1) * H], Xc[c], start=(c == 0), stop=(c == KC - 1))
                leave(mm, 1, "f")
                pe.wait_ge(S("lf_ready"), 2)
                for t in range(3):
                    rows = P if t < 2 else NB
                    pe.transpose(B[5][0:rows, t * H:(t + 1) * H], a.fx[:, t * P:t * P + rows], ident[0:H, 0:H])
                for t in range(2):
                    mm = pe.transpose(B[5][:, (3 + t) * H:(4 + t) * H], a.fe[:, t * P:(t + 1) * P], ident[0:H, 0:H])
                pe.matmul(B[6][0:96, 0:8], cst("rep12", H), a.fx[:, SEQ:T], start=True, stop=True)\
                  .then_inc(S("lf_rows"), 1)
                pe.wait_ge(S("lf_nat"), 3)
                pe.wait_ge(S("lf_rows_copied"), 1)

            def cached_gates(a):
                pe.wait_ge(S("natural_copied"), cnt["natural"])
                pe.wait_ge(S("lf_in"), 16 * PAGES * NB)
                u = a.LF
                for j in range(4):
                    for pg in range(4):
                        mm = pe.transpose(B[j][0:96, pg * P:(pg + 1) * P], u[:, (4 * j + pg) * 96:(4 * j + pg + 1) * 96],
                                          ident)
                    mm.then_inc(S("lf_turned"), 1)
                pe.wait_ge(S("lf_copied"), 4)

            def sample_scores(layer, a):
                pe.wait_ge(S("qz_built"), (a.nk + 1) * (layer + 1) if layer == 0 else (2 + 1) + (4 + 1))
                per = UNIT // a.W
                steps = []
                for u in range(NB * PAGES // per):
                    b, first = divmod(u * per, PAGES)
                    for kv in range(a.nk):
                        for j in range(first // 4, (first + per) // 4):
                            steps.append((u, b, kv, j, first))
                pending = []

                def product(st, n):
                    u, b, kv, j, first = st
                    pe.wait_ge(S("kt_copied"), n)
                    return pe.matmul(B[j][0:96, :], a.Qz[:, (kv * NB + b) * 96:(kv * NB + b + 1) * 96],
                                     a.KTs[:, 512 * (n % 2):512 * (n % 2) + 512],
                                     start=(b == 0 and kv == 0), stop=(b == NB - 1 and kv == a.nk - 1))

                last = None
                for k, st in enumerate(steps):
                    u, b, kv, j, first = st
                    tile = arrived(pe, layer, "k", u) if (k == 0 or steps[k - 1][0] != u) else ring[units[layer]["k", u][0]]
                    n = bump("kt")
                    if n > 2:
                        pe.wait_ge(S("kt_copied"), n - 2)
                    for pg in range(4):
                        at = (4 * j + pg - first) * a.W + kv * P
                        mm = pe.transpose(B[4 + n % 2][:, pg * P:(pg + 1) * P], tile[:, at:at + P], ident)
                    mm.then_inc(S("kt_ready"), 1)
                    if last is not None:
                        mm = product(last, n - 1)
                        if k + 1 == len(steps) or steps[k + 1][0] != u:
                            leave(mm, layer, "k", u)
                    last = st
                product(last, n)
                for b in range(NB):
                    for kv in range(a.nk):
                        mm = pe.matmul(B[6][0:96, 0:1], a.Qz[:, (kv * NB + b) * 96:(kv * NB + b + 1) * 96],
                                       a.kT[:, kv * T + SEQ + b:kv * T + SEQ + b + 1],
                                       start=(b == 0 and kv == 0), stop=(b == NB - 1 and kv == a.nk - 1))
                mm.then_inc(S("k_scores"), 1)

                def mem_product(b, hp, n):
                    pe.wait_ge(S("kt_copied"), n)
                    for s in range(2):
                        h = 2 * hp + s
                        mm = pe.matmul(B[7][32 * s:32 * s + 32, 0:SEQ], a.Qmz[:, (h * NB + b) * 32:(h * NB + b + 1) * 32],
                                       a.KTs[:, 512 * (n % 2) + SEQ * s:512 * (n % 2) + SEQ * (s + 1)],
                                       start=(b == 0 and hp == 0), stop=(b == NB - 1 and hp == 1))
                    return mm

                last = None
                for b in range(NB):
                    tile = arrived(pe, layer, "mk", b // 4) if b % 4 == 0 else ring[units[layer]["mk", b // 4][0]]
                    for hp in range(2):
                        n = bump("kt")
                        pe.wait_ge(S("kt_copied"), n - 2)
                        for s in range(2):
                            for pg in range(2):
                                at = ((b % 4) * 2 + pg) * 512 + (2 * hp + s) * P
                                mm = pe.transpose(B[4 + n % 2][:, (2 * s + pg) * P:(2 * s + pg + 1) * P],
                                                  tile[:, at:at + P], ident)
                        mm.then_inc(S("kt_ready"), 1)
                        if last is not None:
                            mm = mem_product(*last, n - 1)
                            if b % 4 == 3 and hp == 1:
                                leave(mm, layer, "mk", b // 4)
                        last = (b, hp)
                mem_product(*last, n).then_inc(S("km_scores"), 1)
                pe.wait_ge(S("scores_added"), layer + 1)

            def prompt_attention(layer, a):
                base = 16 * layer
                items = [("self", t, hp) for t in range(2) for hp in range(6)] + \
                        [("mem", t, hp) for t in range(2) for hp in range(2)]
                for n in range(len(items) + 3):
                    if n < len(items):
                        kind, t, hp = items[n]
                        if n >= 2:
                            pe.wait_ge(S("p_max"), base + n - 1)
                        for s in range(2):
                            h = 2 * hp + s
                            out = B[n % 2][:, s * SEQ:(s + 1) * SEQ]
                            if kind == "self":
                                kv = h // a.G
                                mm = pe.matmul(out, a.qT[:, h * T + t * P:h * T + (t + 1) * P],
                                               a.kT[:, kv * T:kv * T + SEQ], start=True, stop=(layer == 0))
                                if layer == 1:
                                    mm = pe.matmul(out, ident[0:H, h:h + 1].broadcast_to((H, P)), a.fe[:, 0:SEQ],
                                                   start=False, stop=True)
                            else:
                                mm = pe.matmul(out, a.qmT[:, h * T + t * P:h * T + (t + 1) * P],
                                               a.memK[:, h * SEQ:(h + 1) * SEQ], start=True, stop=True)
                        mm.then_inc(S("p_scores"), 1)
                    if 2 <= n <= len(items) + 1:
                        m = n - 2
                        pe.wait_ge(S("p_norm"), base + m + 1)
                        if m >= 2:
                            pe.wait_ge(S("p_turned_copied"), base + m - 1)
                        for k in range(4):
                            mm = pe.transpose(B[2 + m % 2][:, k * P:(k + 1) * P], a.sc[m % 3][:, k * P:(k + 1) * P], ident)
                        mm.then_inc(S("p_turned"), 1)
                    if n >= 3:
                        m = n - 3
                        kind, t, hp = items[m]
                        pe.wait_ge(S("p_turned_copied"), base + m + 1)
                        if m >= 2:
                            pe.wait_ge(S("p_out_copied"), base + m - 1)
                        for s in range(2):
                            h = 2 * hp + s
                            for g in range(2):
                                v = a.VN[:, g * a.W + (h // a.G) * P:g * a.W + (h // a.G + 1) * P] if kind == "self" \
                                    else a.memV[:, g * 512 + h * P:g * 512 + (h + 1) * P]
                                mm = pe.matmul(B[4 + m % 2][:, s * P:(s + 1) * P], v,
                                               a.PTp[m % 2][:, (2 * s + g) * P:(2 * s + g + 1) * P],
                                               start=(g == 0), stop=(g == 1))
                        mm.then_inc(S("p_out"), 1)
                pe.wait_ge(S("p_out_copied"), base + len(items))

            def sample_attention(layer, a):
                if layer == 0:
                    pe.wait_ge(S("mask_ready"), 1)
                    for j in range(4):
                        pe.matmul(B[j][0:96, :], cst("to12", NB, 96), a.S[96:96 + NB, 512 * j:512 * j + 512],
                                  start=True, stop=True)
                    pe.matmul(B[4][0:96, 0:1], cst("to12", NB, 96), a.S[96:96 + NB, PAST:L1], start=True, stop=True)\
                      .then_inc(S("mask_rows"), 1)
                pe.wait_ge(S("s_norm"), layer + 1)
                for pg in range(PAGES):
                    mm = pe.transpose(B[pg // 5][:, (pg % 5) * 96:(pg % 5 + 1) * 96], a.S[0:96, pg * P:(pg + 1) * P],
                                      ident[0:96, 0:96])
                pe.transpose(B[4][0:NB, 0:96], a.epn, ident[0:96, 0:96])
                for g in range(2):
                    mm = pe.transpose(B[5][:, 32 * g:32 * g + 32], a.Sm[:, g * P:(g + 1) * P], ident[0:32, 0:32])
                mm.then_inc(S("s_turned"), 1)
                pe.wait_ge(S("s_turned_copied"), 6 * (layer + 1))
                per = UNIT // a.W

                def fold_out(b):
                    pe.wait_ge(S("ov_copied"), 12 * layer + b + 1)
                    for kv in range(a.nk):
                        at = (b * a.nk + kv) * H
                        mm = pe.matmul(B[5][:, at:at + H], a.ovs[:, kv * P:(kv + 1) * P], cst("fold12"),
                                       start=True, stop=True)
                    mm.then_inc(S("ov_turned"), 1)

                for b in range(NB):
                    out = B[6 + b % 2]
                    if b >= 2:
                        pe.wait_ge(S("ov_copied"), 12 * layer + b - 1)
                    for u in range(b * PAGES // per, (b + 1) * PAGES // per):
                        tile = arrived(pe, layer, "v", u)
                        for k in range(per):
                            pg = (u * per) % PAGES + k
                            g = pg % 4
                            mm = pe.matmul(out[32 * g:32 * g + 32, 0:a.W], ar(pg * 96 + b * H, 32),
                                           tile[:, k * a.W:(k + 1) * a.W], start=(pg < 4), stop=(pg >= 12 and g > 0))
                        leave(mm, layer, "v", u)
                    pe.matmul(out[0:32, 0:a.W], ar(PAGES * 96 + 64 + b * H, 32, NB), a.VNs, start=False, stop=True)\
                      .then_inc(S("ov_ready"), 1)
                    if b:
                        fold_out(b - 1)
                fold_out(NB - 1)

                def fold_mem(m):
                    pe.wait_ge(S("ov_copied"), 12 * layer + NB + m + 1)
                    for h in range(HM):
                        at = (m * HM + h) * 2 * HM
                        mm = pe.matmul(B[4][:, at:at + 2 * HM], a.ovs[:, h * P:(h + 1) * P], cst("fold4"),
                                       start=True, stop=True)
                    mm.then_inc(S("ov_turned"), 1)

                for m in range(NB // 2):
                    out = B[6 + m % 2]
                    pe.wait_ge(S("ov_copied"), 12 * layer + NB + m - 1)
                    tile = arrived(pe, layer, "mv", m // 2)
                    for j in range(2):
                        for g in range(2):
                            b, q = 2 * m + j, 32 * (2 * j + g)
                            mm = pe.matmul(out[q:q + 32, :], ar(PAGES * 96 + 32 * g + HM * b, 32),
                                           tile[:, ((b % 4) * 2 + g) * 512:((b % 4) * 2 + g + 1) * 512],
                                           start=True, stop=True)
                    mm.then_inc(S("ov_ready"), 1)
                    if m:
                        fold_mem(m - 1)
                fold_mem(NB // 2 - 1)
                for k in range(2):
                    leave(pe.transpose(B[7][:, 0:P], ident, ident), layer, "mv", k)
                pe.wait_ge(S("at_done"), layer + 1)

            def layer_norm(k):
                for c in range(KC):
                    pe.wait_ge(S("mixed"), 16 * k + max(c + 1, 12))
                    mm = pe.matmul(B[0][:, 0:T], cst("mean"), Xc[c], start=(c == 0), stop=(c == KC - 1))
                mm.then_inc(S("ln_mean"), 1)
                for c in range(KC):
                    pe.wait_ge(S("ln_square"), 16 * k + c + 1)
                    pe.matmul(B[1][:, 0:T], cst("mean"), M.sq[c % 2], start=(c == 0), stop=(c == KC - 1))\
                      .then_inc(S("ln_square_used"), 1)

            def router_weights(layer):
                u = arrived(pe, layer, "r")
                for j in range(4):
                    mm = pe.transpose(B[6][:, j * 80:(j + 1) * 80], u[0:80, j:j + 4 * (P - 1) + 1:4], ident[0:80, 0:80])
                leave(mm, layer, "r")

            def token_rows(tiles, last):
                for t in tiles:
                    rows = P if t < 2 else NB
                    for q in range(4):
                        n = bump("token_rows")
                        if 4 * t + q >= 4:
                            pe.wait_ge(S("token_rows_copied" if last else "high_made"), 4 * t + q - 3 if last else n - 4)
                        if last and t == 0:
                            pe.wait_ge(S("ln_out"), 3 * KC + 4 * q + 4)
                        for c in range(4):
                            mm = pe.transpose(B[2 + n % 4][0:rows, c * P:(c + 1) * P],
                                              Xc[4 * q + c][:, t * P:t * P + rows], ident)
                        mm.then_inc(S("token_rows"), 1)

            def experts(layer):
                sm = lambda name: S(f"{name}_l{layer}")
                pe.wait_ge(S("wr_copied"), layer + 1)
                for c in range(KC):
                    pe.wait_ge(S("ln_out"), KC * 2 * layer + c + 1)
                    mm = pe.matmul(B[7][0:20, 0:T], wr[:, 20 * c:20 * c + 20], Xc[c], start=(c == 0), stop=(c == KC - 1))
                mm.then_inc(S("logits"), 1)
                pe.wait_ge(S("logits_copied"), layer + 1)
                for t in range(3):
                    rows = P if t < 2 else NB
                    mm = pe.transpose(B[6][0:rows, 20 * t:20 * t + 20], M.lgT[:, t * P:t * P + rows], ident[0:20, 0:20])
                mm.then_inc(S("logit_rows"), 1)
                token_rows(range(2), False)
                pe.wait_ge(S("chosen"), layer + 1)
                sel = M.w16[0]
                for t in range(4):
                    out = B[7][:, 16 * t:16 * t + 16]
                    for g in range(min(t + 1, 3)):
                        rows = P if g < 2 else NB
                        m = cst("before") if g == t else cst("ones")
                        mm = pe.matmul(out, m[0:rows, :], sel[0:rows, 16 * g:16 * g + 16],
                                       start=(g == 0), stop=(g == min(t, 2)))
                mm.then_inc(S("ranks"), 1)
                token_rows(range(2, 3), False)
                pe.wait_ge(S("low_made"), cnt["token_rows"])
                pe.wait_ge(S("zeroed"), ZERO[2] if layer == 0 else ZERO[4])
                pe.wait_ge(S(f"route_done_l{layer}"), 1)
                n_pair = pe.value_load(npair[0:1, 0:1], min_val=PAIRS, max_val=PAIRS + (MAX_EXTRA + 1) // 2)

                def gather(done):
                    pe.wait_ge(sm("chosen_slots"), done + 1)
                    for q in range(4):
                        if q >= 2:
                            pe.wait_ge(sm("gather_copied"), done * 4 + (q - 1))
                        for c in range(4):
                            for t in range(3):
                                rows = P if t < 2 else NB
                                for k in range(3):
                                    mm = pe.matmul(B[6 + q % 2][:, c * P:(c + 1) * P],
                                                   M.part[t][k][0:rows, (4 * q + c) * P:(4 * q + c + 1) * P],
                                                   M.sel[0:rows, t * P:(t + 1) * P],
                                                   start=(t == 0 and k == 0), stop=(t == 2 and k == 2))
                        mm.then_inc(sm("gathered"), 1)

                def scatter(it, c):
                    if c >= 2:
                        pe.wait_ge(sm("scatter_added"), it * 16 + (c - 1))
                    pe.matmul((B[2] if c % 2 == 0 else B[6])[:, 0:T], M.ys[:, c * P:(c + 1) * P], M.gt,
                              start=True, stop=True).then_inc(sm("scattered"), 1)

                def gate_up(it, first, bank, between):
                    for half in range(2):
                        slots = [moe_unit(layer, first + 2 * half + s, it)[0:2] for s in range(2)]
                        for slot, v in slots:
                            pe.wait_ge(full(layer, slot), v)
                        for c in range(8):
                            for s in range(2):
                                mm = pe.matmul(B[bank][64 * s:64 * s + 64, :],
                                               M.xsT[:, (8 * half + c) * P + 64 * s:(8 * half + c) * P + 64 * s + 64],
                                               ring[slots[s][0]][:, c * FE:(c + 1) * FE],
                                               start=(half == 0 and c == 0), stop=(half == 1 and c == 7))
                                if c == 7:
                                    mm.then_inc(free(layer, slots[s][0]), 1)
                            between(8 * half + c)

                def turn_hidden(it):
                    pe.wait_ge(sm("hidden"), it + 1)
                    for f in range(4):
                        mm = pe.transpose(B[3][:, f * P:(f + 1) * P], M.hh[:, f * P:(f + 1) * P], ident)
                    mm.then_inc(sm("hidden_turned"), 1)

                def down(it):
                    pe.wait_ge(sm("hidden_copied"), it + 1)
                    for q in range(4):
                        slots = [moe_unit(layer, 8 + 2 * (q // 2) + s, it)[0:2] for s in range(2)]
                        if q % 2 == 0:
                            for slot, v in slots:
                                pe.wait_ge(full(layer, slot), v)
                        if q >= 2:
                            pe.wait_ge(sm("rows_out"), it * 4 + q)
                        for f in range(4):
                            for s in range(2):
                                at = f * (D // 2) + (q % 2) * 512
                                mm = pe.matmul(B[4 + q % 2][64 * s:64 * s + 64, :],
                                               M.hT[:, f * P + 64 * s:f * P + 64 * s + 64],
                                               ring[slots[s][0]][:, at:at + 512], start=(f == 0), stop=(f == 3))
                                if f == 3 and q % 2 == 1:
                                    mm.then_inc(free(layer, slots[s][0]), 1)
                        if q % 2 == 0:
                            mm.then_inc(sm("down_ready"), 1)

                gather(0)
                with pe.Fori(0, n_pair) as it:
                    pe.wait_ge(sm("gather_copied"), it * 4 + 4)
                    pe.wait_ge(sm("rows_out"), it * 4 + 1)
                    pe.wait_ge(sm("gt_copied"), it + 1)

                    def with_scatter(k):
                        if k % 2 == 1:
                            scatter(it, k - 1)
                            scatter(it, k)

                    gate_up(it, 0, 0, with_scatter)
                    pe.wait_ge(sm("scatter_added"), it * 16 + 16)
                    for t in range(3):
                        rows = P if t < 2 else NB
                        mm = pe.transpose(B[2][:, t * P:t * P + rows], M.sg[0:rows, t * P:(t + 1) * P],
                                          ident[0:rows, 0:rows])
                    mm.then_inc(sm("gt_ready"), 1)
                    gate_up(it, 4, 1, lambda k: None)
                    gather(it + 1)
                    turn_hidden(it)
                    down(it)
                pe.wait_ge(sm("rows_out"), n_pair * 4 + 1)
                pe.wait_ge(sm("gt_copied"), n_pair + 1)
                pe.wait_ge(sm("gather_copied"), n_pair * 4 + 4)
                for c in range(KC):
                    scatter(n_pair, c)

            t = arrived(pe, 0, "ln")
            pe.transpose(B[5][:, 0:P], t[:, 0:P], ident).then_inc(free(0, units[0]["ln", 0][0]), 1)
            turn_rows(0, "x")
            for layer in range(2):
                a = lay[layer]
                if layer == 0:
                    pe.wait_ge(S("lnp_copied"), 1)
                    indexer(a)
                else:
                    forget_gates(a)
                for k in range(3):
                    slab(layer, "q", k, Xc, T)
                for k in range(1 if layer == 0 else 2):
                    slab(layer, "kv", k, Xc, T)
                slab(layer, "qm", 0, Xc, T)
                slabs_done()
                natural(a.kT, a.nk, 3)
                natural(a.vT, a.nk, 3)
                if layer == 1:
                    cached_gates(a)
                pe.wait_ge(S("natural_copied"), cnt["natural"])
                memory(layer, a)
                sample_scores(layer, a)
                prompt_attention(layer, a)
                sample_attention(layer, a)
                router_weights(layer)
                for k in range(4):
                    g = bump("mix")
                    for half in range(2):
                        u = arrived(pe, layer, "o", 2 * k + half)
                        if k >= 2 and half == 0:
                            pe.wait_ge(S("mixed"), 32 * layer + 4 * (k - 1))
                        bank0 = 4 * (k % 2)
                        if k == 1 and half == 0:
                            pe.wait_ge(S("wr_copied"), layer + 1)
                        for f in range(4):
                            for c in range(8):
                                mm = pe.matmul(B[bank0 + f][:, 0:T], u[:, c * 512 + f * P:c * 512 + (f + 1) * P],
                                               Ac[8 * half + c], start=(half == 0 and c == 0),
                                               stop=(half == 1 and c == 7))
                        leave(mm, layer, "o", 2 * k + half)
                layer_norm(2 * layer)
                experts(layer)
                layer_norm(2 * layer + 1)
            token_rows(range(3), True)

        stores = [0]

        @block.scalar
        def _(act):
            cnt = {}

            def bump(name, k=1):
                cnt[name] = cnt.get(name, 0) + k
                return cnt[name]

            def copy(out, in_, scale=1.0):
                return act.activation(out, in_, ACT.Copy, scale=scale)

            def store(dst, src):
                stores[0] += 1
                act.dma_start(dst, src).then_inc(S("stored"), 16)

            def turn_rows(dst, n_tok):
                for c in range(KC):
                    n = bump("rows")
                    act.wait_ge(S("rows_turned"), n)
                    copy(dst[c][:, 0:n_tok], B[n % 4][:, 0:n_tok]).then_inc(S("rows_copied"), 1)

            def slab(layer, name, k, dsts, n_tok, scale=1.0):
                g = bump("slab")
                left(act, layer, name, 2 * k + 1)
                for f in range(4):
                    c = copy(dsts[f], B[4 * (g % 2) + f][:, 0:n_tok], scale)
                c.then_inc(S("slab_copied"), 1)

            def natural(dsts, w):
                for rows, dst in dsts:
                    n = bump("natural")
                    act.wait_ge(S("natural_ready"), n)
                    copy(dst, B[4 + n % 2][0:rows, 0:w]).then_inc(S("natural_copied"), 1)

            def heads(t, n, w=T):
                return [t[:, k * w:(k + 1) * w] for k in range(n)]

            def indexer(a):
                left(act, 0, "kiwi")
                copy(a.KI, B[4][:, 0:T]).then_inc(S("kiwi_copied"), 1)
                copy(a.WI, B[5][0:IH, 0:T], IH ** -0.5).then_inc(S("kiwi_copied"), 1)
                act.wait_ge(S("kiwi_rows"), 1)
                copy(a.nat[:, 0:P], B[6][:, 0:P]).then_inc(S("kiwi_rows_copied"), 1)
                copy(a.nat[0:NB, P:192], B[6][0:NB, P:192]).then_inc(S("kiwi_rows_copied"), 1)
                copy(a.nat[:, 192:224], B[6][:, 192:224]).then_inc(S("kiwi_rows_copied"), 1)
                act.wait_ge(S("kiwi_rows_copied"), 3)
                store(o["a_ik_p"][0, 0].rearrange("(t p) d -> p t d", p=P),
                      a.nat[:, 0:P].rearrange("p (t d) -> p t d", t=2))
                store(o["a_ik_s"][0].rearrange("b a d -> (b a) d"), a.nat[0:NB, P:192])
                for k in range(2):
                    load_ik(range(0, 3) if k == 0 else range(3, IK_EARLY))
                    slab(0, "qi", k, heads(a.qiT[:, k * 4 * T:(k + 1) * 4 * T], 4), T)
                act.wait_ge(S("zeroed"), ZERO[0])
                act.wait_ge(S("slab_copied"), 2)
                q = a.qiT[:, 0:8 * T].rearrange("p (c t) -> p c t", t=T)[:, :, SEQ:T]
                for s in range(2):
                    dst = diagonal(a.QIz, s, 64 * s, 64, [(2, 8), (P + IH, NB)])
                    copy(dst, q[64 * s:64 * s + 64]).then_inc(S("qiz_built"), 1)
                for n in range(16):
                    act.wait_ge(S("ixp_scores"), n + 1)
                    if n >= 2:
                        act.wait_ge(S("ixp_added"), n - 1)
                    for s in range(2):
                        r = act.activation(a.RL[:, 512 * (n % 2) + SEQ * s:512 * (n % 2) + SEQ * (s + 1)],
                                           B[4 + 2 * (n % 2) + s][:, 0:SEQ], ACT.Relu, scale=64 ** -0.5)
                    r.then_inc(S("ixp_relu"), 1)

                def relu(j):
                    w = 512 if j < 4 else 1
                    act.wait_ge(S("ix_scores"), j + 1)
                    if j:
                        act.wait_ge(S("ix_rows"), j)
                    act.activation(a.tb[:, 0:w], (B[2 + j % 2] if j < 4 else B[4])[:, 0:w], ACT.Relu,
                                   scale=64 ** -0.5).then_inc(S("ix_relu"), 1)

                def rows(j):
                    w = 512 if j < 4 else 1
                    act.wait_ge(S("ix_rows"), j + 1)
                    copy(a.S[96:96 + NB, 512 * j:512 * j + w], B[5][96:96 + NB, 0:w]).then_inc(S("ix_rows_copied"), 1)

                for n in range(32):
                    bump("kt")
                    act.wait_ge(S("kt_ready"), n + 1)
                    copy(a.KTs[:, 512 * (n % 2):512 * (n % 2) + 512], B[n % 2][:, :]).then_inc(S("kt_copied"), 1)
                    if n % NB == 0 and n:
                        relu(n // NB - 1)
                    if n % NB == 1 and n > 1:
                        rows(n // NB - 1)
                relu(3)
                rows(3)
                relu(4)
                rows(4)

            def diagonal(tile, offset, p0, rows, dims):
                v = tile[p0:p0 + rows, offset:offset + 1]
                return bass.AP(tensor=v.tensor, offset=v.offset, ap=[list(v.ap[0])] + [[s, n] for s, n in dims])

            def forget_gates(a):
                left(act, 1, "f")
                act.wait_ge(S("bias_in"), 80)
                act.activation(a.fx, B[4][0:H, 0:T], ACT.Identity, bias=fbias[:, 0:1]).then_inc(S("f_biased"), 1)
                act.wait_ge(S("f_abs"), 1)
                act.activation(a.fe, a.fe, ACT.Exp, scale=-1.0).then_inc(S("f_exp"), 1)
                act.wait_ge(S("f_exp"), 1)
                act.activation(a.fe, a.fe, ACT.Ln, bias=1.0).then_inc(S("f_ln"), 1)
                act.wait_ge(S("lf_rows"), 1)
                copy(a.lfn[:, 0:2 * H], B[5][:, 0:2 * H]).then_inc(S("lf_nat"), 1)
                copy(a.lfn[0:NB, 2 * H:3 * H], B[5][0:NB, 2 * H:3 * H]).then_inc(S("lf_nat"), 1)
                copy(a.cq, B[5][:, 3 * H:5 * H], -1.0).then_inc(S("lf_nat"), 1)
                act.wait_ge(S("lf_nat"), 3)
                store(o["b_lf_p"][0, 0].rearrange("(t p) d -> p t d", p=P),
                      a.lfn[:, 0:2 * H].rearrange("p (t d) -> p t d", t=2))
                store(o["b_lf_s"][0].rearrange("b a d -> (b a) d"), a.lfn[0:NB, 2 * H:3 * H])

            def pad_queries(layer, a):
                act.wait_ge(S("zeroed"), ZERO[1] if layer == 0 else ZERO[3])
                act.wait_ge(S("slab_copied"), cnt["slab"])
                for kv in range(a.nk):
                    src = a.qT[:, :].rearrange("p (h t) -> p h t", t=T)[:, kv * a.G:(kv + 1) * a.G, SEQ:T]
                    copy(diagonal(a.Qz, kv * NB * 96 + a.G * kv, 0, P, [(1, a.G), (96 + H, NB)]), src)\
                        .then_inc(S("qz_built"), 1)
                src = a.qmT[:, :].rearrange("p (h t) -> p h t", t=T)[:, :, SEQ:T]
                copy(diagonal(a.Qmz, 0, 0, P, [(NB * 32 + 1, HM), (32 + 4, NB)]), src).then_inc(S("qz_built"), 1)

            def sample_scores(layer, a):
                steps = NB * a.nk * 4 + 2 * NB
                for _ in range(steps):
                    n = bump("kt")
                    act.wait_ge(S("kt_ready"), n)
                    copy(a.KTs[:, 512 * (n % 2):512 * (n % 2) + 512], B[4 + n % 2][:, :]).then_inc(S("kt_copied"), 1)

            def prompt_attention(layer, a):
                base = 16 * layer
                items = [("self", t, hp) for t in range(2) for hp in range(6)] + \
                        [("mem", t, hp) for t in range(2) for hp in range(2)]
                nm, rs = a.st[:, 0:6], a.st[:, 6:12]
                for n in range(len(items) + 3):
                    if n < len(items):
                        act.wait_ge(S("p_max"), base + n + 1)
                        for s in range(2):
                            x = a.sc[n % 3][:, SEQ * s:SEQ * (s + 1)]
                            k = 2 * (n % 3) + s
                            e = act.activation(x, x, ACT.Exp, bias=nm[:, k:k + 1], accum_out=rs[:, k:k + 1])
                        e.then_inc(S("p_exp"), 1)
                    if 2 <= n <= len(items) + 1:
                        m = n - 2
                        act.wait_ge(S("p_turned"), base + m + 1)
                        if m >= 2:
                            act.wait_ge(S("p_out"), base + m - 1)
                        copy(a.PTp[m % 2], B[2 + m % 2][:, :]).then_inc(S("p_turned_copied"), 1)
                    if n >= 3:
                        m = n - 3
                        kind, t, hp = items[m]
                        h = 2 * hp + (0 if kind == "self" else H)
                        act.wait_ge(S("p_out"), base + m + 1)
                        copy(Av[:, h:h + 2, t * P:(t + 1) * P],
                             B[4 + m % 2][:, 0:SEQ].rearrange("p (h t) -> p h t", h=2)).then_inc(S("p_out_copied"), 1)

            def sample_attention(layer, a):
                nm, rs = a.st[:, 8:10], a.st[:, 10:12]
                act.wait_ge(S("s_max"), layer + 1)
                act.activation(a.S[0:96, 0:L1], a.S[0:96, 0:L1], ACT.Exp, bias=nm[0:96, 0:1],
                               accum_out=rs[0:96, 0:1])
                act.activation(a.Sm, a.Sm, ACT.Exp, bias=nm[0:32, 1:2], accum_out=rs[0:32, 1:2])\
                   .then_inc(S("s_exp"), 1)
                act.wait_ge(S("s_turned"), layer + 1)
                for k in range(4):
                    w = 480 if k < 3 else 96
                    copy(a.PT[:, 480 * k:480 * k + w], B[k][:, 0:w]).then_inc(S("s_turned_copied"), 1)
                copy(a.PTn, B[4][0:NB, 0:96]).then_inc(S("s_turned_copied"), 1)
                copy(a.PTm, B[5][:, 0:64]).then_inc(S("s_turned_copied"), 1)
                for m in range(NB + NB // 2):
                    act.wait_ge(S("ov_ready"), 12 * layer + m + 1)
                    if m:
                        act.wait_ge(S("ov_turned"), 12 * layer + m)
                    w = a.W if m < NB else 512
                    copy(a.ovs[:, 0:w], B[6 + m % 2][:, 0:w]).then_inc(S("ov_copied"), 1)
                act.wait_ge(S("ov_turned"), 12 * layer + 12)
                for kv in range(a.nk):
                    src = B[5][:, 0:NB * a.nk * H].rearrange("p (b k h) -> p k h b", k=a.nk, h=H)
                    copy(Av[:, kv * a.G:(kv + 1) * a.G, SEQ:T], src[:, kv, kv * a.G:(kv + 1) * a.G, :])
                src = diagonal(B[4], 0, 0, P, [(2 * HM + 1, HM), (2 * HM * HM, NB // 2), (HM, 2)])
                copy(Av[:, H:H + HM, SEQ:T].rearrange("p h (m j) -> p h m j", j=2), src).then_inc(S("at_done"), 1)

            def layer_norm(k):
                layer, j = divmod(k, 2)
                for c in range(KC):
                    act.wait_ge(S("ln_centred"), 16 * k + c + 1)
                    if 16 * k + c >= 2:
                        act.wait_ge(S("ln_square_used"), 16 * k + c - 1)
                    act.activation(M.sq[c % 2], Xc[c], ACT.Square).then_inc(S("ln_square"), 1)
                act.wait_ge(S("ln_var"), k + 1)
                act.activation(M.rstd, M.rstd, ACT.Sqrt).then_inc(S("ln_std"), 1)
                for c in range(KC):
                    act.wait_ge(S("ln_normed"), 16 * k + c + 1)
                    g = 64 * j + 16 * layer + c
                    act.activation(Xc[c], Xc[c], ACT.Identity, bias=lnp[:, g + 32:g + 33], scale=lnp[:, g:g + 1])\
                       .then_inc(S("ln_out"), 1)

            def token_rows():
                for t in range(3):
                    rows = P if t < 2 else NB
                    for q in range(4):
                        n = bump("token_rows")
                        act.wait_ge(S("token_rows"), n)
                        copy(M.xtok[0:rows, t * D + 512 * q:t * D + 512 * (q + 1)], B[2 + n % 4][0:rows, :])\
                            .then_inc(S("token_rows_copied"), 1)
                    act.wait_ge(S("token_rows_copied"), 4 * t + 4)
                    dst = o["y_prompt"][0, t * P:(t + 1) * P, :] if t < 2 else o["y_sample"].rearrange("b a d -> (b a) d")
                    store(dst, M.xtok[0:rows, t * D:(t + 1) * D])

            def row_parts(layer, steps):
                for n in steps:
                    if n <= 12:
                        rows, _, out = row_item(n)
                        act.wait_ge(S("token_rows"), bump("token_rows"))
                        if n > 4:
                            act.wait_ge(S("low_made"), 12 * layer + n - 4)
                        copy(M.rest[n % 4][0:rows, :], B[2 + n % 4][0:rows, :])
                        copy(out[0], B[2 + n % 4][0:rows, :]).then_inc(S("high_made"), 1)
                    if n > 1:
                        rows, _, out = row_item(n - 1)
                        act.wait_ge(S("rest_made"), 12 * layer + n - 1)
                        copy(out[1], M.rest[(n - 1) % 4][0:rows, :]).then_inc(S("mid_made"), 1)

            def experts(layer):
                sm = lambda name: S(f"{name}_l{layer}")
                act.wait_ge(S("bias_in"), 80)
                act.wait_ge(S("logits"), layer + 1)
                act.activation(M.lgT, B[7][0:20, 0:T], ACT.Identity, bias=rbias[:, layer:layer + 1])\
                   .then_inc(S("logits_copied"), 1)
                for k in range(2):
                    row_parts(layer, range(1 + 2 * k, 3 + 2 * k))
                    act.wait_ge(S("r_shifted"), 2 * layer + k + 1)
                    act.activation(M.a4[k], M.a4[k], ACT.Exp).then_inc(S("r_exp"), 1)
                row_parts(layer, range(5, 14))
                act.wait_ge(S(f"route_done_l{layer}"), 1)
                n_pair = act.value_load(npair[0:1, 0:1], min_val=PAIRS, max_val=PAIRS + (MAX_EXTRA + 1) // 2)

                def gather_copies(done):
                    for q in range(4):
                        act.wait_ge(sm("gathered"), done * 4 + (q + 1))
                        copy(M.xsT[:, 512 * q:512 * (q + 1)], B[6 + q % 2][:, :]).then_inc(sm("gather_copied"), 1)

                def exp_gate(it):
                    for k in (2, 3):
                        slot, _, v = moe_unit(layer, k, it)
                        act.wait_ge(free(layer, slot), v)
                    act.activation(M.ex, B[0][:, :], ACT.Exp, scale=-1.0).then_inc(sm("gate_exp"), 1)

                def hidden_copy(it):
                    act.wait_ge(sm("hidden_turned"), it + 1)
                    copy(M.hT, B[3][:, :]).then_inc(sm("hidden_copied"), 1)

                def rows_out(it):
                    for q in range(4):
                        if q % 2 == 0:
                            act.wait_ge(sm("down_ready"), it * 2 + (q // 2 + 1))
                        else:
                            for s in range(2):
                                slot, _, v = moe_unit(layer, 8 + q - 1 + s, it)
                                act.wait_ge(free(layer, slot), v)
                        copy(M.ys[:, 512 * q:512 * (q + 1)], B[4 + q % 2][:, :]).then_inc(sm("rows_out"), 1)

                act.wait_ge(sm("rows_out"), 1)
                act.wait_ge(sm("gt_copied"), 1)
                gather_copies(0)
                with act.Fori(0, n_pair) as it:
                    exp_gate(it)
                    act.wait_ge(sm("gt_ready"), it + 1)
                    copy(M.gt, B[2][:, 0:T]).then_inc(sm("gt_copied"), 1)
                    gather_copies(it + 1)
                    hidden_copy(it)
                    rows_out(it)

            act.wait_ge(S("table_in"), 16)
            pregs = [act.alloc_register(f"act_page{k}") for k in range(8)]

            def load_ik(seqs):
                for b in seqs:
                    load_pages(act, pregs, S("ik_in"), b, 0, PAGES, i["cache_a_ik"][0],
                               lambda g: lay[0].IK[:, (b * PAGES + g) * 64:(b * PAGES + g + 1) * 64])

            def load_lf(seqs):
                for b in seqs:
                    load_pages(act, pregs, S("lf_in"), b, 0, PAGES, i["cache_b_lf"][0],
                               lambda g: lay[1].LF[:, g * 96 + b * H:g * 96 + (b + 1) * H])

            left(act, 0, "ln")
            copy(lnp[:, :], B[5][:, 0:P]).then_inc(S("lnp_copied"), 1)
            turn_rows(Xc, T)
            for layer in range(2):
                a = lay[layer]
                if layer == 0:
                    indexer(a)
                else:
                    forget_gates(a)
                for k in range(3):
                    if layer == 1:
                        load_lf(range(2 * k, 2 * k + 2))
                    slab(layer, "q", k, heads(a.qT[:, k * 4 * T:(k + 1) * 4 * T], 4), T, SCALE)
                if layer == 0:
                    slab(layer, "kv", 0, heads(a.kT, 2) + heads(a.vT, 2), T)
                else:
                    load_lf(range(6, NB))
                    slab(layer, "kv", 0, heads(a.kT, 4), T)
                    slab(layer, "kv", 1, heads(a.vT, 4), T)
                slab(layer, "qm", 0, heads(a.qmT, 4), T, SCALE)
                pre = "a" if layer == 0 else "b"
                KN = a.KN[:, 0:2 * a.W].rearrange("p (t w) -> p t w", t=2)
                VN = a.VN.rearrange("p (t w) -> p t w", t=2)
                natural([(P, KN[:, 0, :]), (P, KN[:, 1, :]), (NB, a.KNs[:, 0:a.W])], a.W)
                act.wait_ge(S("natural_copied"), cnt["natural"])
                store(o[pre + "_k_p"][0, 0].rearrange("(t p) k d -> p t (k d)", p=P), KN)
                store(o[pre + "_k_s"][0].rearrange("b a k d -> (b a) (k d)"), a.KNs[:, 0:a.W])
                natural([(P, VN[:, 0, :]), (P, VN[:, 1, :]), (NB, a.VNs)], a.W)
                act.wait_ge(S("natural_copied"), cnt["natural"])
                store(o[pre + "_v_p"][0, 0].rearrange("(t p) k d -> p t (k d)", p=P), VN)
                store(o[pre + "_v_s"][0].rearrange("b a k d -> (b a) (k d)"), a.VNs)
                if layer == 1:
                    for j in range(4):
                        act.wait_ge(S("lf_turned"), j + 1)
                        copy(a.S[0:96, 512 * j:512 * j + 512], B[j][0:96, :]).then_inc(S("lf_copied"), 1)
                turn_rows(Ac, SEQ)
                slab(layer, "mkv", 0, heads(a.memK, 4, SEQ), SEQ)
                slab(layer, "mkv", 1, heads(a.mvT, 4, SEQ), SEQ)
                act.wait_ge(S("stored"), 16 * stores[0])
                if layer == 0:
                    act.wait_ge(S("ixp_added"), 16)
                MN = a.KN.rearrange("p (t w) -> p t w", t=2)
                MV = a.memV.rearrange("p (t w) -> p t w", t=2)
                natural([(P, MN[:, 0, :]), (P, MN[:, 1, :])], 512)
                natural([(P, MV[:, 0, :]), (P, MV[:, 1, :])], 512)
                act.wait_ge(S("natural_copied"), cnt["natural"])
                store(o["mem_k_p"][layer, 0].rearrange("(t p) k d -> p t (k d)", p=P), MN)
                store(o["mem_v_p"][layer, 0].rearrange("(t p) k d -> p t (k d)", p=P), MV)
                act.sem_inc(S("memory_done"), 1)
                pad_queries(layer, a)
                act.wait_ge(S("stored"), 16 * stores[0])
                sample_scores(layer, a)
                prompt_attention(layer, a)
                sample_attention(layer, a)
                left(act, layer, "r")
                copy(wr[:, :].rearrange("p (c a j) -> p c a j", a=5, j=4),
                     B[6][:, 0:320].rearrange("p (j a c) -> p c a j", a=5, c=KC)).then_inc(S("wr_copied"), 1)
                layer_norm(2 * layer)
                experts(layer)
                layer_norm(2 * layer + 1)
            token_rows()

        @block.vector
        def _(dve):
            chain = [0]

            def link(ins):
                chain[0] += 1
                ins.then_inc(S("dve_chain"), 1)
                dve.wait_ge(S("dve_chain"), chain[0])

            def top_k(sc, m8, k):
                for _ in range(k // 8):
                    link(dve.max(m8, sc))
                    link(dve.match_replace(sc, m8, sc, TAKEN))

            def prompt_index(a):
                for n in range(16):
                    t, c = divmod(n, 8)
                    dve.wait_ge(S("ixp_relu"), n + 1)
                    if n == 0:
                        dve.wait_ge(S("kiwi_rows_copied"), 3)
                    acc = a.MASK[:, t * SEQ:(t + 1) * SEQ]
                    for s in range(2):
                        w = a.nat[:, 192 + IH * t + 2 * c + s:193 + IH * t + 2 * c + s]
                        rl = a.RL[:, 512 * (n % 2) + SEQ * s:512 * (n % 2) + SEQ * (s + 1)]
                        if c == 0 and s == 0:
                            link(dve.tensor_scalar(acc, rl, w, None, ALU.mult))
                        elif s == 0:
                            link(dve.scalar_tensor_tensor(acc, rl, w, acc, ALU.mult, ALU.add))
                        else:
                            dve.scalar_tensor_tensor(acc, rl, w, acc, ALU.mult, ALU.add)\
                               .then_inc(S("ixp_added"), 1)
                            dve.wait_ge(S("ixp_added"), n + 1)

            def sample_topk(a):
                dve.wait_ge(S("ix_rows_copied"), 5)
                sc = a.S[96:96 + NB, 0:L1]
                top_k(sc, a.m8[96:96 + NB, :], TOPK_S)
                dve.tensor_scalar(sc, sc, -2e38, NEG, ALU.is_gt, ALU.mult).then_inc(S("mask_ready"), 1)

            def prompt_topk(a):
                for t in range(2):
                    m = a.MASK[:, t * SEQ:(t + 1) * SEQ]
                    causal = cst("causal")[:, t * SEQ:(t + 1) * SEQ]
                    link(dve.tensor_tensor(m, m, causal, ALU.add))
                    top_k(m, a.m8, TOPK_P)
                    link(dve.tensor_scalar(m, m, -2e38, NEG, ALU.is_gt, ALU.mult))
                    link(dve.tensor_tensor(m, m, causal, ALU.add))

            def forget_gates(a):
                dve.wait_ge(S("f_biased"), 1)
                dve.scalar_tensor_tensor(a.fe, a.fx, -1.0, a.fx, ALU.mult, ALU.max).then_inc(S("f_abs"), 1)
                dve.wait_ge(S("f_abs"), 1)
                dve.wait_ge(S("f_ln"), 1)
                link(dve.tensor_scalar(a.fx, a.fx, 0.0, None, ALU.min))
                link(dve.tensor_tensor(a.fx, a.fx, a.fe, ALU.subtract))
                dve.sem_inc(S("lf_ready"), 1)
                zero = cst("causal", H)[:, 0:1].broadcast_to((H, SEQ))
                link(dve.tensor_tensor_scan(a.fe[:, 0:SEQ], a.fx[:, 0:SEQ], zero, 0.0, ALU.add, ALU.add))
                link(dve.tensor_scalar(a.fe[:, 0:SEQ], a.fe[:, 0:SEQ], -1.0, None, ALU.mult))
                dve.sem_inc(S("lf_ready"), 1)
                dve.wait_ge(S("lf_rows"), 1)
                link(dve.tensor_tensor(a.own, B[6][0:96, 0:8], cst("own12", 96), ALU.mult))
                link(dve.tensor_reduce(a.st[0:96, 12:13], a.own, AX.X, ALU.add))
                dve.sem_inc(S("lf_rows_copied"), 1)

            def cached_gates(a):
                dve.wait_ge(S("lf_copied"), 4)
                link(dve.tensor_copy(a.S[0:96, PAST:L1], a.st[0:96, 12:13]))
                zero = cst("causal", 96)[:, 0:1].broadcast_to((96, L1))
                link(dve.tensor_tensor_scan(a.S[0:96, 0:L1], a.S[0:96, 0:L1], zero, 0.0, ALU.add, ALU.add))
                link(dve.tensor_copy(a.st[0:96, 13:14], a.S[0:96, PAST:L1]))
                link(dve.tensor_scalar(a.S[0:96, 0:L1], a.S[0:96, 0:L1], -1.0, a.st[0:96, 13:14], ALU.mult, ALU.add))

            def add_scores(layer, a):
                if layer == 0:
                    arrived(dve, 0, "ln")
                dve.wait_ge(S("k_scores"), layer + 1)
                for j in range(4):
                    r = a.S[0:96, 512 * j:512 * j + 512]
                    link(dve.tensor_tensor(r, B[j][0:96, :], r, ALU.add))
                link(dve.tensor_tensor(a.S[0:96, PAST:L1], B[6][0:96, 0:1], a.S[0:96, PAST:L1], ALU.add))
                dve.wait_ge(S("km_scores"), layer + 1)
                link(dve.tensor_copy(a.Sm, B[7][0:32, 0:SEQ]))
                link(dve.tensor_tensor(a.Sm, a.Sm, B[7][32:64, 0:SEQ], ALU.add))
                dve.sem_inc(S("scores_added"), 1)

            def prompt_attention(layer, a):
                base = 16 * layer
                items = [("self", t, hp) for t in range(2) for hp in range(6)] + \
                        [("mem", t, hp) for t in range(2) for hp in range(2)]
                nm, rs = a.st[:, 0:6], a.st[:, 6:12]
                slope = slopes()
                for n in range(len(items) + 1):
                    if n < len(items):
                        kind, t, hp = items[n]
                        sc, ps = a.sc[n % 3], B[n % 2]
                        if kind == "self" and layer == 0:
                            for s in range(2):
                                link(dve.scalar_tensor_tensor(a.tb[:, s * SEQ:(s + 1) * SEQ],
                                                              cst("dist")[:, t * SEQ:(t + 1) * SEQ],
                                                              -float(np.float32(slope[2 * hp + s])),
                                                              a.MASK[:, t * SEQ:(t + 1) * SEQ], ALU.mult, ALU.add))
                        dve.wait_ge(S("p_scores"), base + n + 1)
                        if n >= 3:
                            dve.wait_ge(S("p_turned"), base + n - 2)
                        if kind == "mem":
                            link(dve.tensor_copy(sc, ps[:, :]))
                        elif layer == 0:
                            link(dve.tensor_tensor(sc, ps[:, :], a.tb, ALU.add))
                        else:
                            for s in range(2):
                                k = t * H + 2 * hp + s
                                link(dve.scalar_tensor_tensor(sc[:, s * SEQ:(s + 1) * SEQ],
                                                              ps[:, s * SEQ:(s + 1) * SEQ], a.cq[:, k:k + 1],
                                                              cst("causal")[:, t * SEQ:(t + 1) * SEQ],
                                                              ALU.add, ALU.add))
                        k = 2 * (n % 3)
                        dve.tensor_reduce(nm[:, k:k + 2], sc.rearrange("p (s k) -> p s k", s=2), AX.X, ALU.max,
                                          negate=True).then_inc(S("p_max"), 1)
                    if n >= 1:
                        m = n - 1
                        k = 2 * (m % 3)
                        dve.wait_ge(S("p_exp"), base + m + 1)
                        link(dve.reciprocal(rs[:, k:k + 2], rs[:, k:k + 2]))
                        for s in range(2):
                            x = a.sc[m % 3][:, s * SEQ:(s + 1) * SEQ]
                            e = dve.tensor_scalar(x, x, rs[:, k + s:k + s + 1], None, ALU.mult)
                        e.then_inc(S("p_norm"), 1)

            def sample_attention(layer, a):
                nm, rs = a.st[:, 8:10], a.st[:, 10:12]
                S_ = a.S[0:96, 0:L1]
                if layer == 0:
                    dve.wait_ge(S("mask_rows"), 1)
                    for j in range(4):
                        r = a.S[0:96, 512 * j:512 * j + 512]
                        link(dve.tensor_tensor(r, B[j][0:96, :], r, ALU.add))
                    link(dve.tensor_tensor(a.S[0:96, PAST:L1], B[4][0:96, 0:1], a.S[0:96, PAST:L1], ALU.add))
                link(dve.tensor_reduce(nm[0:96, 0:1], S_, AX.X, ALU.max, negate=True))
                dve.tensor_reduce(nm[0:32, 1:2], a.Sm, AX.X, ALU.max, negate=True).then_inc(S("s_max"), 1)
                dve.wait_ge(S("s_exp"), layer + 1)
                link(dve.reciprocal(rs[0:96, 0:1], rs[0:96, 0:1]))
                link(dve.reciprocal(rs[0:32, 1:2], rs[0:32, 1:2]))
                link(dve.tensor_scalar(S_, S_, rs[0:96, 0:1], None, ALU.mult))
                link(dve.tensor_scalar(a.Sm, a.Sm, rs[0:32, 1:2], None, ALU.mult))
                dve.tensor_scalar(a.epn, cst("own12", 96), a.S[0:96, PAST:L1], None, ALU.mult)\
                   .then_inc(S("s_norm"), 1)

            def mix(layer):
                for k in range(4):
                    left(dve, layer, "o", 2 * k + 1)
                    for f in range(4):
                        c = 4 * k + f
                        dve.scalar_tensor_tensor(Xc[c], Xc[c], ALPHA, B[4 * (k % 2) + f][:, 0:T], ALU.mult, ALU.add)\
                           .then_inc(S("mixed"), 1)

            def layer_norm(k):
                dve.wait_ge(S("ln_mean"), k + 1)
                dve.wait_ge(S("mixed"), 16 * (k + 1))
                for c in range(KC):
                    dve.tensor_tensor(Xc[c], Xc[c], B[0][:, 0:T], ALU.subtract).then_inc(S("ln_centred"), 1)
                dve.wait_ge(S("ln_square_used"), 16 * (k + 1))
                dve.tensor_scalar(M.rstd, B[1][:, 0:T], EPS, None, ALU.add).then_inc(S("ln_var"), 1)
                dve.wait_ge(S("ln_std"), k + 1)
                link(dve.reciprocal(M.rstd, M.rstd))
                for c in range(KC):
                    dve.tensor_tensor(Xc[c], Xc[c], M.rstd, ALU.mult).then_inc(S("ln_normed"), 1)

            def route(layer):
                v3 = lambda x, n: x.rearrange("p (t k) -> p t k", k=n)
                b3 = lambda x, n: x.unsqueeze(2).broadcast_to((P, 3, n))
                dve.wait_ge(S("logit_rows"), layer + 1)
                dve.wait_ge(S("zeroed"), ZERO[2] if layer == 0 else ZERO[4])
                link(dve.tensor_copy(M.lg[:, 0:40], B[6][:, 0:40]))
                link(dve.tensor_copy(M.lg[0:NB, 40:60], B[6][0:NB, 40:60]))
                lg = v3(M.lg, 20)
                gp, ep, og, t4, o1, o2, tmp, el = [v3(x, 4) for x in M.a4]
                mx, sm_, pg, v2, w1, w2, den, f1 = M.c1[0:8]
                first = v3(cst("first"), 4)

                def one_hot(out, x, m):
                    link(dve.tensor_tensor(t4, x, b3(m, 4), ALU.is_equal))
                    link(dve.tensor_tensor(t4, t4, first, ALU.mult))
                    link(dve.tensor_reduce(f1, t4, AX.X, ALU.max))
                    link(dve.tensor_tensor(out, t4, b3(f1, 4), ALU.is_equal))

                link(dve.tensor_reduce(mx, lg[:, :, 0:4], AX.X, ALU.max))
                dve.tensor_tensor(gp, lg[:, :, 0:4], b3(mx, 4), ALU.subtract).then_inc(S("r_shifted"), 1)
                dve.wait_ge(S("r_exp"), 2 * layer + 1)
                link(dve.tensor_reduce(sm_, gp, AX.X, ALU.add))
                link(dve.tensor_reduce(mx, gp, AX.X, ALU.max))
                link(dve.reciprocal(pg, sm_))
                link(dve.tensor_tensor(pg, pg, mx, ALU.mult))
                one_hot(og, gp, mx)
                for g in range(4):
                    e = lg[:, :, 4 + 4 * g:8 + 4 * g]
                    w = og[:, :, g:g + 1].broadcast_to((P, 3, 4))
                    link(dve.tensor_tensor(el if g == 0 else tmp, e, w, ALU.mult))
                    if g:
                        link(dve.tensor_tensor(el, el, tmp, ALU.add))
                link(dve.tensor_reduce(mx, el, AX.X, ALU.max))
                dve.tensor_tensor(ep, el, b3(mx, 4), ALU.subtract).then_inc(S("r_shifted"), 1)
                dve.wait_ge(S("r_exp"), 2 * layer + 2)
                link(dve.tensor_reduce(mx, ep, AX.X, ALU.max))
                one_hot(o1, ep, mx)
                link(dve.scalar_tensor_tensor(ep, o1, -2.0, ep, ALU.mult, ALU.add))
                link(dve.tensor_reduce(v2, ep, AX.X, ALU.max))
                one_hot(o2, ep, v2)
                link(dve.tensor_tensor(den, mx, v2, ALU.add))
                link(dve.reciprocal(den, den))
                link(dve.tensor_tensor(den, den, pg, ALU.mult))
                link(dve.tensor_tensor(w1, mx, den, ALU.mult))
                link(dve.tensor_tensor(w2, v2, den, ALU.mult))
                link(dve.tensor_tensor(tmp, o1, b3(w1, 4), ALU.mult))
                link(dve.tensor_tensor(t4, o2, b3(w2, 4), ALU.mult))
                link(dve.tensor_tensor(tmp, tmp, t4, ALU.add))
                link(dve.tensor_tensor(o1, o1, o2, ALU.add))
                link(dve.tensor_tensor(o1, o1, b3(cst("valid"), 4), ALU.mult))
                sel, gate, slot = M.w16[0], M.w16[1], M.w16[2]
                for g in range(4):
                    w = og[:, :, g:g + 1].broadcast_to((P, 3, 4))
                    link(dve.tensor_tensor(v3(sel, 16)[:, :, 4 * g:4 * g + 4], o1, w, ALU.mult))
                    link(dve.tensor_tensor(v3(gate, 16)[:, :, 4 * g:4 * g + 4], tmp, w, ALU.mult))
                dve.sem_inc(S("chosen"), 1)
                dve.wait_ge(S("ranks"), layer + 1)
                link(dve.scalar_tensor_tensor(slot, B[7][:, 0:48], 1.0, sel, ALU.add, ALU.mult))
                link(dve.tensor_scalar(slot, slot, -1.0, None, ALU.add))
                link(dve.tensor_copy(M.cnt, B[7][:, 48:64]))
                n_ec, nx = NE * CHUNKS, ENTRIES - NE
                fl, pos, ord_, tmp64 = [x[:, 0:n_ec] for x in M.fl]
                cb = M.cnt.unsqueeze(2).broadcast_to((P, NE, CHUNKS))
                e2 = lambda x: x.rearrange("p (e c) -> p e c", c=CHUNKS)
                link(dve.tensor_tensor(e2(fl), cb, e2(cst("chunk_base")), ALU.is_gt))
                zero = cst("causal")[:, 0:1].broadcast_to((P, n_ec))
                link(dve.tensor_tensor_scan(pos, fl, zero, 0.0, ALU.add, ALU.add))
                link(dve.tensor_tensor(ord_, pos, fl, ALU.mult))
                link(dve.tensor_scalar(ord_, ord_, -1.0, None, ALU.add))
                ind = M.ind.rearrange("p (k j) -> p k j", j=n_ec)
                link(dve.tensor_tensor(ind, ord_.unsqueeze(1).broadcast_to((P, nx, n_ec)),
                                       cst("entry").unsqueeze(2).broadcast_to((P, nx, n_ec)), ALU.is_equal))
                link(dve.tensor_scalar(tmp64, cst("chunk_base"), -BIG, None, ALU.add))
                link(dve.memset(M.LB[:, 0:NE], 0.0))
                link(dve.tensor_copy(M.LE, cst("entry_expert")))
                link(dve.tensor_tensor(ind, ind, tmp64.unsqueeze(1).broadcast_to((P, nx, n_ec)), ALU.mult))
                link(dve.tensor_reduce(M.LB[:, NE:ENTRIES], ind, AX.X, ALU.add))
                link(dve.tensor_scalar(M.LB[:, NE:ENTRIES], M.LB[:, NE:ENTRIES], BIG, None, ALU.add))
                link(dve.tensor_tensor(ind, ord_.unsqueeze(1).broadcast_to((P, nx, n_ec)),
                                       cst("entry").unsqueeze(2).broadcast_to((P, nx, n_ec)), ALU.is_equal))
                link(dve.tensor_tensor(ind, ind, cst("chunk_expert").unsqueeze(1).broadcast_to((P, nx, n_ec)), ALU.mult))
                link(dve.tensor_reduce(M.LE[:, NE:ENTRIES], ind, AX.X, ALU.add))
                link(dve.tensor_copy(ent[:, :], M.LE[0:1, :]))
                half = (MAX_EXTRA + 1) // 2
                for k in range(half):
                    link(dve.tensor_scalar(M.no[0:1, k:k + 1], pos[0:1, n_ec - 1:n_ec], 2.0 * k, None, ALU.is_gt))
                link(dve.tensor_reduce(M.no[0:1, 7:8], M.no[0:1, 0:half], AX.X, ALU.add))
                link(dve.tensor_scalar(npair[:, :], M.no[0:1, 7:8], float(PAIRS), None, ALU.add))
                dve.sem_inc(S(f"route_done_l{layer}"), 1)

            def experts(layer):
                sm = lambda name: S(f"{name}_l{layer}")
                route(layer)
                n_pair = dve.value_load(npair[0:1, 0:1], min_val=PAIRS, max_val=PAIRS + (MAX_EXTRA + 1) // 2)
                gate, slot = M.w16[1], M.w16[2]
                regs = [dve.alloc_register(f"expert{k}_l{layer}") for k in range(2)]
                v3 = lambda x, n: x.rearrange("p (t k) -> p t k", k=n)

                class Links:
                    per, base, n = LINKS_PER_PASS, 0, 0

                lk = Links()

                def link(ins, done):
                    lk.n += 1
                    ins.then_inc(sm("pass_chain"), 1)
                    dve.wait_ge(sm("pass_chain"), done * lk.per + (lk.base + lk.n))

                def choose(done, k):
                    dve.reg_load(regs, ent[0:1, bass.ds(k * 2, 2)] if not isinstance(k, int) else ent[0:1, 2 * k:2 * k + 2])
                    ee = [dve.snap(g, min_val=0, max_val=NE - 1) for g in regs]
                    for s in range(2):
                        lb = M.LB[:, bass.ds(k * 2 + s, 1)]
                        link(dve.tensor_scalar(M.d3[:, 3 * s:3 * s + 3].unsqueeze(2), v3(slot, 16)[:, :, bass.ds(ee[s], 1)],
                                               lb, None, ALU.subtract), done)
                        out = M.sel.rearrange("p (t k) -> p t k", k=P)[:, :, 64 * s:64 * s + 64]
                        link(dve.tensor_tensor(out, cst("slot").unsqueeze(1).broadcast_to((P, 3, CAP)),
                                               M.d3[:, 3 * s:3 * s + 3].unsqueeze(2).broadcast_to((P, 3, CAP)),
                                               ALU.is_equal), done)
                        sg = M.sg.rearrange("p (t k) -> p t k", k=P)[:, :, 64 * s:64 * s + 64]
                        link(dve.tensor_tensor(sg, out,
                                               v3(gate, 16)[:, :, bass.ds(ee[s], 1)].broadcast_to((P, 3, CAP)),
                                               ALU.mult), done)
                    dve.tensor_copy(M.no[:, 0:1], M.no[:, 1:2]).then_inc(sm("chosen_slots"), 1)

                def scatter_add(it, c):
                    dve.wait_ge(sm("scattered"), it * 16 + (c + 1))
                    b = B[2] if c % 2 == 0 else B[6]
                    dve.tensor_tensor(Ac[c], b[:, 0:T], Ac[c], ALU.add).then_inc(sm("scatter_added"), 1)

                def hidden(it):
                    dve.wait_ge(sm("gate_exp"), it + 1)
                    link(dve.tensor_scalar(M.ex, M.ex, 1.0, None, ALU.add), it)
                    link(dve.reciprocal(M.ex, M.ex), it)
                    link(dve.tensor_tensor(M.ex, B[0][:, :], M.ex, ALU.mult), it)
                    for k in (6, 7):
                        slot_, _, v = moe_unit(layer, k, it)
                        dve.wait_ge(free(layer, slot_), v)
                    dve.tensor_tensor(M.hh, B[1][:, :], M.ex, ALU.mult).then_inc(sm("hidden"), 1)

                link(dve.memset(M.no, 0.0), 0)
                choose(0, 0)
                lk.base, lk.n = lk.n, 0
                with dve.Fori(0, n_pair) as it:
                    for c in range(KC):
                        scatter_add(it, c)
                    dve.wait_ge(sm("gt_ready"), it + 1)
                    choose(it, it + 1)
                    hidden(it)
                assert lk.n == LINKS_PER_PASS, lk.n
                for c in range(KC):
                    scatter_add(n_pair, c)
                dve.wait_ge(sm("scatter_added"), n_pair * 16 + 16)
                for c in range(KC):
                    dve.scalar_tensor_tensor(Xc[c], Xc[c], ALPHA, Ac[c], ALU.mult, ALU.add).then_inc(S("mixed"), 1)

            dve.wait_ge(S("consts_in"), 16)
            for layer in range(2):
                a = lay[layer]
                if layer == 0:
                    dve.wait_ge(S("wblock"), 1)
                    dve.tensor_tensor(a.Wb, B[7][:, 0:NB], cst("own16"), ALU.mult).then_inc(S("wblock_copied"), 1)
                    prompt_index(a)
                    sample_topk(a)
                    prompt_topk(a)
                else:
                    forget_gates(a)
                    cached_gates(a)
                add_scores(layer, a)
                prompt_attention(layer, a)
                sample_attention(layer, a)
                mix(layer)
                layer_norm(2 * layer)
                experts(layer)
                layer_norm(2 * layer + 1)
        assert stores[0] == N_STORES, stores[0]


QI_AT = H * P + 2 * 256
N_STORES = 2 + 4 + 2 + 2 + 4 + 2 + 3
LINKS_PER_PASS = 9

_INS = ['x_prompt', 'x_sample', 'mem_prompt', 'cache_a_k', 'cache_a_v', 'cache_a_ik', 'cache_b_k', 'cache_b_v',
        'cache_b_lf', 'cache_mem_k', 'cache_mem_v', 'page_table', 'w_in_a', 'w_in_b', 'b_f', 'w_mem_kv', 'w_o',
        'ln1_g', 'ln1_b', 'ln2_g', 'ln2_b', 'w_r1', 'b_r1', 'w_r2', 'b_r2', 'w_gate', 'w_up', 'w_down']
_OUTS = [("y_prompt", (1, SEQ, D)), ("y_sample", (NB, 1, D)),
         ("a_k_p", (1, 1, SEQ, 2, P)), ("a_v_p", (1, 1, SEQ, 2, P)), ("a_ik_p", (1, 1, SEQ, 64)),
         ("b_k_p", (1, 1, SEQ, 4, P)), ("b_v_p", (1, 1, SEQ, 4, P)), ("b_lf_p", (1, 1, SEQ, H)),
         ("mem_k_p", (2, 1, 256, HM, P)), ("mem_v_p", (2, 1, 256, HM, P)),
         ("a_k_s", (1, NB, 1, 2, P)), ("a_v_s", (1, NB, 1, 2, P)), ("a_ik_s", (1, NB, 1, 64)),
         ("b_k_s", (1, NB, 1, 4, P)), ("b_v_s", (1, NB, 1, 4, P)), ("b_lf_s", (1, NB, 1, H))]


def kernel(**inputs):
    import concourse.bacc as bacc
    from concourse.bass_utils import run_bass_kernel_spmd

    nc = bacc.Bacc("TRN2", target_bir_lowering=False, num_devices=1)
    arrays, i, o = {}, {}, {}
    given = {name: inputs[name] for name in _INS}
    given["consts"] = CONSTS
    given["alibi"] = alibi_rows()
    for name, a in given.items():
        a = np.ascontiguousarray(a)
        arrays[f"in_{name}"] = a
        i[name] = nc.dram_tensor(f"in_{name}", a.shape, mybir.dt.from_np(a.dtype), kind="ExternalInput").ap()
    for name, shape in _OUTS:
        o[name] = nc.dram_tensor(f"out_{name}", shape, F32, kind="ExternalOutput").ap()
    step_kernel(nc, i, o)
    r = run_bass_kernel_spmd(nc, [arrays], core_ids=[0])
    return tuple(r.results[0][f"out_{name}"] for name, _ in _OUTS)
```
